# Optimizing a Trainium2 kernel written in Bass

```python
import math
import jax, jax.numpy as jnp
from jax import lax
import numpy as np

D_MODEL = 1024
BATCH = 1
SEQ = 256
DEPTH = 1

N_MIXERS = 3
N_LAYERS_A = len(range(0, DEPTH, N_MIXERS))
N_LAYERS_B = len(range(1, DEPTH, N_MIXERS))
N_LAYERS_C = len(range(2, DEPTH, N_MIXERS))

DEEPNORM_ALPHA = (2.0 * DEPTH) ** 0.25
DEEPNORM_BETA = (8.0 * DEPTH) ** -0.25
LN_EPS = 1e-5

A_HEADS = 8
A_HEAD_DIM = D_MODEL // A_HEADS
MOBA_BLOCK = 256
MOBA_TOPK = 3
MOBA_Q_CHUNK = 16
REL_BUCKETS = 32
REL_MAX_DIST = 128

B_GROUPS = 8
B_WIDTH = 2 * D_MODEL
B_CHUNK = 128

C_HEADS = 4
C_KEY_DIM = D_MODEL // 2
C_VAL_DIM = D_MODEL
C_DK = C_KEY_DIM // C_HEADS
C_DV = C_VAL_DIM // C_HEADS
C_GATE_RANK = 16
C_GATE_NORMALIZER = 16.0
C_CHUNK = 64
C_IN_WIDTH = 2 * C_KEY_DIM + 2 * C_VAL_DIM + C_GATE_RANK

N_EXPERTS = 32
TOP_K = 4
D_EXPERT = D_MODEL
SWIGLU_LIMIT = 7.0
SWIGLU_ALPHA = 1.702
MOE_ROW_BLOCK = 128


def layer_norm(x, g, b):
    xf = x.astype(jnp.float32)
    mu = xf.mean(-1, keepdims=True)
    var = jnp.square(xf - mu).mean(-1, keepdims=True)
    y = (xf - mu) * lax.rsqrt(var + LN_EPS) * g.astype(jnp.float32) + b.astype(jnp.float32)
    return y.astype(x.dtype)

def rms_norm(x, g):
    xf = x.astype(jnp.float32)
    return xf * lax.rsqrt(jnp.mean(xf * xf, -1, keepdims=True) + LN_EPS) * g.astype(jnp.float32)

def t5_bucket(rel):
    n = jnp.maximum(rel, 0)
    max_exact = REL_BUCKETS // 2
    nf = jnp.maximum(n, 1).astype(jnp.float32)
    large = max_exact + (jnp.log(nf / max_exact) / math.log(REL_MAX_DIST / max_exact)
                         * (REL_BUCKETS - max_exact)).astype(jnp.int32)
    large = jnp.minimum(large, REL_BUCKETS - 1)
    return jnp.where(n < max_exact, n, large)

def moba_attention(x, w_in, w_out, rel_bias):
    B, S, _ = x.shape
    H, Dh, BLK, QC = A_HEADS, A_HEAD_DIM, MOBA_BLOCK, MOBA_Q_CHUNK
    qkv = (x @ w_in).reshape(B, S, 3, H, Dh)
    q = qkv[:, :, 0].transpose(0, 2, 1, 3)
    k = qkv[:, :, 1].transpose(0, 2, 1, 3)
    v = qkv[:, :, 2].transpose(0, 2, 1, 3)
    nb = -(-S // BLK)
    pad = nb * BLK - S
    kb = jnp.pad(k, ((0, 0), (0, 0), (0, pad), (0, 0))).reshape(B, H, nb, BLK, Dh)
    vb = jnp.pad(v, ((0, 0), (0, 0), (0, pad), (0, 0))).reshape(B, H, nb, BLK, Dh)
    k_mean = kb.astype(jnp.float32).mean(axis=3)
    gate = jnp.einsum('bhsd,bhnd->bhsn', q.astype(jnp.float32), k_mean)
    pos = jnp.arange(S)
    past = jnp.arange(nb)[None, :] < (pos // BLK)[:, None]
    gate = jnp.where(past, gate, -jnp.inf)
    k_sel = min(MOBA_TOPK, nb)
    sel_score, sel_idx = lax.top_k(gate, k_sel)
    sel_valid = jnp.isfinite(sel_score)

    rel_t = rel_bias.T
    bi = jnp.arange(B)[:, None, None, None]
    hi = jnp.arange(H)[None, :, None, None]
    scale = Dh ** -0.5
    offs = jnp.arange(BLK)

    def attend_chunk(t0):
        qc = lax.dynamic_slice_in_dim(q, t0, QC, axis=2)
        idx = lax.dynamic_slice_in_dim(sel_idx, t0, QC, axis=2)
        valid = lax.dynamic_slice_in_dim(sel_valid, t0, QC, axis=2)
        qpos = t0 + jnp.arange(QC)
        kg = kb[bi, hi, idx]
        vg = vb[bi, hi, idx]
        s_sel = jnp.einsum('bhqd,bhqnjd->bhqnj', qc, kg).astype(jnp.float32) * scale
        rel_sel = qpos[None, None, :, None, None] - (idx[..., None] * BLK + offs)
        s_sel = jnp.where(valid[..., None],
                          s_sel + rel_t[hi[..., None], t5_bucket(rel_sel)], -jnp.inf)
        own = t0 // BLK
        ko = lax.dynamic_index_in_dim(kb, own, axis=2, keepdims=False)
        vo = lax.dynamic_index_in_dim(vb, own, axis=2, keepdims=False)
        rel_own = qpos[:, None] - (own * BLK + offs)[None, :]
        s_own = (jnp.einsum('bhqd,bhjd->bhqj', qc, ko).astype(jnp.float32) * scale
                 + rel_t[:, t5_bucket(rel_own)])
        s_own = jnp.where(rel_own >= 0, s_own, -jnp.inf)
        logits = jnp.concatenate([s_sel.reshape(B, H, QC, k_sel * BLK), s_own], axis=-1)
        p = jax.nn.softmax(logits, axis=-1).astype(v.dtype)
        p_sel = p[..., :k_sel * BLK].reshape(B, H, QC, k_sel, BLK)
        p_own = p[..., k_sel * BLK:]
        return (jnp.einsum('bhqnj,bhqnjd->bhqd', p_sel, vg)
                + jnp.einsum('bhqj,bhjd->bhqd', p_own, vo))

    o = lax.map(attend_chunk, jnp.arange(0, S, QC))
    o = o.transpose(1, 0, 3, 2, 4).reshape(B, S, H * Dh)
    return o @ w_out

def gmlp_mixer(x, w_in, ln_g, ln_b, w_s, b_s, w_out):
    B, S, _ = x.shape
    z = jax.nn.gelu(x @ w_in, approximate=False)
    u, v = jnp.split(z, 2, axis=-1)
    v = layer_norm(v, ln_g, ln_b)
    gw = B_WIDTH // B_GROUPS
    vc = v.reshape(B, S // B_CHUNK, B_CHUNK, B_GROUPS, gw)
    ws = w_s * jnp.tril(jnp.ones((B_CHUNK, B_CHUNK), w_s.dtype))
    mixed = jnp.einsum('gts,bcsge->bctge', ws, vc) + b_s.T[None, None, :, :, None]
    y = u * mixed.reshape(B, S, B_WIDTH)
    return y @ w_out

def gla_mixer(x, w_in, w_gk_up, b_gk, norm_g, w_out):
    B, S, _ = x.shape
    proj = x @ w_in
    splits = [C_KEY_DIM, 2 * C_KEY_DIM, 2 * C_KEY_DIM + C_VAL_DIM, 2 * C_KEY_DIM + 2 * C_VAL_DIM]
    q, k, v, g, gk_low = jnp.split(proj, splits, axis=-1)
    log_a = jax.nn.log_sigmoid((gk_low @ w_gk_up + b_gk).astype(jnp.float32)) / C_GATE_NORMALIZER
    nc = S // C_CHUNK

    def heads(t, dh):
        return t.astype(jnp.float32).reshape(B, nc, C_CHUNK, C_HEADS, dh).transpose(1, 0, 3, 2, 4)

    qh = heads(q, C_DK) * (C_DK ** -0.5)
    kh = heads(k, C_DK)
    vh = heads(v, C_DV)
    ah = heads(log_a, C_DK)
    causal = jnp.tril(jnp.ones((C_CHUNK, C_CHUNK), bool))

    def step(state, inp):
        qc, kc, vc, ac = inp
        b = jnp.cumsum(ac, axis=2)
        o_inter = jnp.einsum('bhck,bhkv->bhcv', qc * jnp.exp(b), state)
        diff = b[:, :, :, None, :] - b[:, :, None, :, :]
        diff = jnp.where(causal[None, None, :, :, None], diff, -jnp.inf)
        att = jnp.einsum('bhik,bhjk,bhijk->bhij', qc, kc, jnp.exp(diff))
        o_intra = jnp.einsum('bhij,bhjv->bhiv', att, vc)
        b_last = b[:, :, -1:, :]
        new_state = (jnp.exp(b_last[:, :, 0, :])[..., None] * state
                     + jnp.einsum('bhck,bhcv->bhkv', kc * jnp.exp(b_last - b), vc))
        return new_state, o_inter + o_intra

    state0 = jnp.zeros((B, C_HEADS, C_DK, C_DV), jnp.float32)
    _, o = lax.scan(step, state0, (qh, kh, vh, ah))
    o = o.transpose(1, 0, 3, 2, 4).reshape(B, S, C_HEADS, C_DV)
    o = rms_norm(o, norm_g) * jax.nn.silu(g.reshape(B, S, C_HEADS, C_DV).astype(jnp.float32))
    return o.reshape(B, S, C_VAL_DIM).astype(x.dtype) @ w_out

def moe_ffn(x, w_router, b_router, w_gu, b_gu, w_down, b_down):
    B, S, D = x.shape
    T = B * S
    xt = x.reshape(T, D)
    logits = (xt @ w_router + b_router).astype(jnp.float32)
    top_logit, top_e = lax.top_k(logits, TOP_K)
    gate = jax.nn.softmax(top_logit, axis=-1)
    n_assign = T * TOP_K
    flat_e = top_e.reshape(-1)
    flat_tok = jnp.arange(n_assign) // TOP_K
    order = jnp.argsort(flat_e)
    e_sorted = flat_e[order]
    tok_sorted = flat_tok[order]
    gate_sorted = gate.reshape(-1)[order]
    counts = jnp.zeros((N_EXPERTS,), jnp.int32).at[flat_e].add(1)
    padded = (counts + MOE_ROW_BLOCK - 1) // MOE_ROW_BLOCK * MOE_ROW_BLOCK
    start = jnp.cumsum(counts) - counts
    pend = jnp.cumsum(padded)
    pstart = pend - padded
    dest = pstart[e_sorted] + (jnp.arange(n_assign) - start[e_sorted])
    n_blocks = -(-n_assign // MOE_ROW_BLOCK) + N_EXPERTS
    n_rows = n_blocks * MOE_ROW_BLOCK
    row_tok = jnp.full((n_rows,), T, jnp.int32).at[dest].set(tok_sorted)
    x_pad = jnp.concatenate([xt, jnp.zeros((1, D), xt.dtype)], axis=0)
    xs = x_pad[row_tok].reshape(n_blocks, MOE_ROW_BLOCK, D)
    block_e = jnp.minimum(
        jnp.searchsorted(pend, jnp.arange(n_blocks) * MOE_ROW_BLOCK, side='right'), N_EXPERTS - 1)

    def expert_block(args):
        xb, e = args
        h = xb @ w_gu[e] + b_gu[e]
        h_gate, h_up = jnp.split(h, 2, axis=-1)
        h_gate = jnp.minimum(h_gate, SWIGLU_LIMIT)
        h_up = jnp.clip(h_up, -SWIGLU_LIMIT, SWIGLU_LIMIT)
        act = h_gate * jax.nn.sigmoid(SWIGLU_ALPHA * h_gate) * (h_up + 1.0)
        return act @ w_down[e] + b_down[e]

    ys = lax.map(expert_block, (xs, block_e)).reshape(n_rows, D)
    y_assign = ys[dest] * gate_sorted[:, None].astype(ys.dtype)
    y = jax.ops.segment_sum(y_assign, tok_sorted, num_segments=T)
    return y.reshape(B, S, D)

def first_inputs(seed: int = 0) -> dict:
    key = jax.random.key(seed)
    ks = jax.random.split(key, 23)
    f32 = jnp.float32
    D = D_MODEL

    def nrm(k, shape, scale):
        return jax.random.normal(k, shape, f32) * scale

    return {
        "x": nrm(ks[0], (BATCH, SEQ, D), 1.0),
        "rel_bias": nrm(ks[1], (REL_BUCKETS, A_HEADS), 0.5),
        "a_w_in": nrm(ks[2], (N_LAYERS_A, D, 3 * D), D ** -0.5),
        "a_w_out": nrm(ks[3], (N_LAYERS_A, D, D), D ** -0.5 * DEEPNORM_BETA),
        "b_w_in": nrm(ks[4], (N_LAYERS_B, D, 2 * B_WIDTH), D ** -0.5),
        "b_ln_g": 1.0 + nrm(ks[5], (N_LAYERS_B, B_WIDTH), 0.02),
        "b_ln_b": nrm(ks[6], (N_LAYERS_B, B_WIDTH), 0.02),
        "b_w_s": nrm(ks[7], (N_LAYERS_B, B_GROUPS, B_CHUNK, B_CHUNK), B_CHUNK ** -0.5),
        "b_b_s": 1.0 + nrm(ks[8], (N_LAYERS_B, B_GROUPS, B_CHUNK), 0.02),
        "b_w_out": nrm(ks[9], (N_LAYERS_B, B_WIDTH, D), B_WIDTH ** -0.5 * DEEPNORM_BETA),
        "c_w_in": nrm(ks[10], (N_LAYERS_C, D, C_IN_WIDTH), D ** -0.5),
        "c_w_gk_up": nrm(ks[11], (N_LAYERS_C, C_GATE_RANK, C_KEY_DIM), C_GATE_RANK ** -0.5),
        "c_b_gk": nrm(ks[12], (N_LAYERS_C, C_KEY_DIM), 0.1),
        "c_norm_g": 1.0 + nrm(ks[13], (N_LAYERS_C, C_DV), 0.02),
        "c_w_out": nrm(ks[14], (N_LAYERS_C, C_VAL_DIM, D), C_VAL_DIM ** -0.5 * DEEPNORM_BETA),
        "ln_g": 1.0 + nrm(ks[15], (DEPTH, 2, D), 0.02),
        "ln_b": nrm(ks[16], (DEPTH, 2, D), 0.02),
        "moe_w_router": nrm(ks[17], (DEPTH, D, N_EXPERTS), D ** -0.5),
        "moe_b_router": nrm(ks[18], (DEPTH, N_EXPERTS), 0.01),
        "moe_w_gate_up": nrm(ks[19], (DEPTH, N_EXPERTS, D, 2 * D_EXPERT), D ** -0.5),
        "moe_b_gate_up": nrm(ks[20], (DEPTH, N_EXPERTS, 2 * D_EXPERT), 0.01),
        "moe_w_down": nrm(ks[21], (DEPTH, N_EXPERTS, D_EXPERT, D), D_EXPERT ** -0.5 * DEEPNORM_BETA),
        "moe_b_down": nrm(ks[22], (DEPTH, N_EXPERTS, D), 0.01),
    }

def first_block(x, rel_bias, a_w_in, a_w_out, b_w_in, b_ln_g, b_ln_b, b_w_s, b_b_s, b_w_out,
              c_w_in, c_w_gk_up, c_b_gk, c_norm_g, c_w_out, ln_g, ln_b,
              moe_w_router, moe_b_router, moe_w_gate_up, moe_b_gate_up, moe_w_down, moe_b_down):
    h = x
    for i in range(DEPTH):
        j = i // N_MIXERS
        mixer = i % N_MIXERS
        if mixer == 0:
            t = moba_attention(h, a_w_in[j], a_w_out[j], rel_bias)
        elif mixer == 1:
            t = gmlp_mixer(h, b_w_in[j], b_ln_g[j], b_ln_b[j], b_w_s[j], b_b_s[j], b_w_out[j])
        else:
            t = gla_mixer(h, c_w_in[j], c_w_gk_up[j], c_b_gk[j], c_norm_g[j], c_w_out[j])
        h = layer_norm(DEEPNORM_ALPHA * h + t, ln_g[i, 0], ln_b[i, 0])
        f = moe_ffn(h, moe_w_router[i], moe_b_router[i], moe_w_gate_up[i], moe_b_gate_up[i],
                    moe_w_down[i], moe_b_down[i])
        h = layer_norm(DEEPNORM_ALPHA * h + f, ln_g[i, 1], ln_b[i, 1])
    return h


MIX_WIDTH = D_MODEL
HGRN_WIDTH = MIX_WIDTH // 2
HGRN_HEADS = 4
HGRN_HEAD_DIM = HGRN_WIDTH // HGRN_HEADS
CONV_WIDTH = MIX_WIDTH - HGRN_WIDTH
CONV_GROUPS = 8
CONV_K = 3
FFN_CONV_K = 3
D_FF = 2816
CHUNK = 64
EPS = 1e-6
IN_COLS = 4 * HGRN_WIDTH + 3 * CONV_WIDTH


def rmsnorm(x, g):
    xf = x.astype(jnp.float32)
    y = xf * lax.rsqrt(jnp.mean(xf * xf, axis=-1, keepdims=True) + EPS)
    return (y * g.astype(jnp.float32)).astype(x.dtype)

def causal_dwconv(x, w):
    k = w.shape[0]
    c = x.shape[-1]
    return lax.conv_general_dilated(
        x, w[:, None, :].astype(x.dtype), window_strides=(1,), padding=[(k - 1, 0)],
        dimension_numbers=("NWC", "WIO", "NWC"), feature_group_count=c)

def to_chunks(t):
    b, t_len, _ = t.shape
    t = t.reshape(b, t_len // CHUNK, CHUNK, HGRN_HEADS, HGRN_HEAD_DIM)
    return t.transpose(1, 0, 3, 2, 4)

def from_chunks(t):
    n, b, h, c, d = t.shape
    return t.transpose(1, 0, 3, 2, 4).reshape(b, n * c, h * d)

def hgrn2_chunkwise(q, k, v, log_f):
    bsz = q.shape[0]
    causal = jnp.tril(jnp.ones((CHUNK, CHUNK), dtype=bool))

    def step(state, inp):
        qc, kc, vc, gc = inp
        b = jnp.cumsum(gc, axis=-2)
        diff = b[..., :, None, :] - b[..., None, :, :]
        decay = jnp.exp(jnp.where(causal[:, :, None], diff, -jnp.inf))
        scores = jnp.einsum('bhtk,bhsk,bhtsk->bhts', qc, kc, decay)
        o = (jnp.einsum('bhts,bhsv->bhtv', scores, vc)
             + jnp.einsum('bhtk,bhkv->bhtv', qc * jnp.exp(b), state))
        b_last = b[..., -1:, :]
        state = (jnp.exp(b_last[..., 0, :])[..., None] * state
                 + jnp.einsum('bhsk,bhsv->bhkv', kc * jnp.exp(b_last - b), vc))
        return state, o

    s0 = jnp.zeros((bsz, HGRN_HEADS, HGRN_HEAD_DIM, HGRN_HEAD_DIM), jnp.float32)
    _, o = lax.scan(step, s0, (to_chunks(q), to_chunks(k), to_chunks(v), to_chunks(log_f)))
    return from_chunks(o)

def hgrn2_mixer(q_pre, f_pre, i_pre, g_pre, lb, norm_g):
    dt = q_pre.dtype
    fp = f_pre.astype(jnp.float32)
    lbf = lb.astype(jnp.float32)
    q = jax.nn.silu(q_pre.astype(jnp.float32)) * (HGRN_HEAD_DIM ** -0.5)
    log_f = jnp.logaddexp(jnp.log(lbf), jnp.log1p(-lbf) + jax.nn.log_sigmoid(fp))
    k = (1.0 - lbf) * jax.nn.sigmoid(-fp)
    v = i_pre.astype(jnp.float32)
    o = hgrn2_chunkwise(q, k, v, log_f)
    bsz, t_len, _ = o.shape
    oh = o.reshape(bsz, t_len, HGRN_HEADS, HGRN_HEAD_DIM)
    oh = oh * lax.rsqrt(jnp.mean(oh * oh, axis=-1, keepdims=True) + EPS)
    o = oh.reshape(bsz, t_len, HGRN_WIDTH) * norm_g.astype(jnp.float32)
    return (o * jax.nn.silu(g_pre.astype(jnp.float32))).astype(dt)

def second_inputs(seed: int = 0) -> dict:
    key = jax.random.key(seed)
    ks = jax.random.split(key, 14)
    f32 = jnp.float32

    def gain(k, shape):
        return 1.0 + 0.05 * jax.random.normal(k, shape, f32)

    return {
        "x": jax.random.normal(ks[0], (BATCH, SEQ, D_MODEL), f32),
        "lb_param": jax.random.normal(ks[1], (DEPTH, HGRN_WIDTH), f32),
        "w_in": jax.random.normal(ks[2], (DEPTH, D_MODEL, IN_COLS), f32) * D_MODEL ** -0.5,
        "w_out": jax.random.normal(ks[3], (DEPTH, MIX_WIDTH, D_MODEL), f32) * MIX_WIDTH ** -0.5,
        "conv_w": jax.random.normal(ks[4], (DEPTH, CONV_K, CONV_WIDTH), f32) * CONV_K ** -0.5,
        "ffn_w_up": jax.random.normal(ks[5], (DEPTH, D_MODEL, 2 * D_FF), f32) * D_MODEL ** -0.5,
        "ffn_conv_w": jax.random.normal(ks[6], (DEPTH, FFN_CONV_K, 2 * D_FF), f32) * FFN_CONV_K ** -0.5,
        "ffn_w_down": jax.random.normal(ks[7], (DEPTH, D_FF, D_MODEL), f32) * D_FF ** -0.5,
        "hgrn_norm_g": gain(ks[8], (DEPTH, HGRN_WIDTH)),
        "pre_mix_g": gain(ks[9], (DEPTH, D_MODEL)),
        "post_mix_g": gain(ks[10], (DEPTH, D_MODEL)),
        "pre_ffn_g": gain(ks[11], (DEPTH, D_MODEL)),
        "post_ffn_g": gain(ks[12], (DEPTH, D_MODEL)),
    }

def second_block(x, lb_param, w_in, w_out, conv_w, ffn_w_up, ffn_conv_w, ffn_w_down,
              hgrn_norm_g, pre_mix_g, post_mix_g, pre_ffn_g, post_ffn_g):
    lb_all = jnp.cumsum(jax.nn.softmax(lb_param.astype(jnp.float32), axis=0), axis=0)
    lb_all = lb_all - lb_all[0:1]
    split_pts = [HGRN_WIDTH * j for j in range(1, 5)] + [4 * HGRN_WIDTH + CONV_WIDTH * j for j in range(1, 3)]

    for l in range(DEPTH):
        h = rmsnorm(x, pre_mix_g[l])
        z = jnp.einsum('btd,dc->btc', h, w_in[l])
        q_p, f_p, i_p, g_p, gate_b, gate_c, conv_h = jnp.split(z, split_pts, axis=-1)
        mix_a = hgrn2_mixer(q_p, f_p, i_p, g_p, lb_all[l], hgrn_norm_g[l])
        mix_b = gate_b * causal_dwconv(gate_c * conv_h, conv_w[l])
        mix = jnp.einsum('btc,cd->btd', jnp.concatenate([mix_a, mix_b], axis=-1), w_out[l])
        x = x + rmsnorm(mix, post_mix_g[l])
        h = rmsnorm(x, pre_ffn_g[l])
        u = causal_dwconv(jnp.einsum('btd,df->btf', h, ffn_w_up[l]), ffn_conv_w[l])
        gate, val = jnp.split(u, 2, axis=-1)
        y = jnp.einsum('btf,fd->btd', jax.nn.silu(gate) * val, ffn_w_down[l])
        x = x + rmsnorm(y, post_ffn_g[l])
    return x


def setup_inputs(seed=0):
    out = dict(first_inputs(seed))
    for name, value in second_inputs(seed + 1).items():
        if name != "x":
            out[name + "_2"] = value
    return out


def reference(
    x, rel_bias, a_w_in, a_w_out, b_w_in, b_ln_g, b_ln_b, b_w_s, b_b_s, b_w_out, c_w_in,
    c_w_gk_up, c_b_gk, c_norm_g, c_w_out, ln_g, ln_b, moe_w_router, moe_b_router, moe_w_gate_up,
    moe_b_gate_up, moe_w_down, moe_b_down, lb_param_2, w_in_2, w_out_2, conv_w_2, ffn_w_up_2,
    ffn_conv_w_2, ffn_w_down_2, hgrn_norm_g_2, pre_mix_g_2, post_mix_g_2, pre_ffn_g_2,
    post_ffn_g_2,
):
    x = first_block(
        x, rel_bias, a_w_in, a_w_out, b_w_in, b_ln_g, b_ln_b, b_w_s, b_b_s, b_w_out, c_w_in,
        c_w_gk_up, c_b_gk, c_norm_g, c_w_out, ln_g, ln_b, moe_w_router, moe_b_router,
        moe_w_gate_up, moe_b_gate_up, moe_w_down, moe_b_down,
    )
    return second_block(
        x, lb_param_2, w_in_2, w_out_2, conv_w_2, ffn_w_up_2, ffn_conv_w_2, ffn_w_down_2,
        hgrn_norm_g_2, pre_mix_g_2, post_mix_g_2, pre_ffn_g_2, post_ffn_g_2,
    )


_drawn_inputs = setup_inputs


def setup_inputs(seed=0):
    import zlib

    import numpy as np

    out = dict(_drawn_inputs(seed))
    spreads = {}
    factors = {'moe_b_gate_up': 8.0, 'moe_b_down': 7.851, 'hgrn_norm_g_2': 2.713}
    for name, (base, spread) in spreads.items():
        noise = np.random.default_rng([zlib.crc32(name.encode()), seed]).standard_normal(out[name].shape)
        drawn = base * np.exp(spread * noise) if base else spread * noise
        out[name] = __import__('jax').numpy.asarray(drawn.astype(out[name].dtype))
    for name, factor in factors.items():
        out[name] = (out[name] * factor).astype(out[name].dtype)
    return out
```

```python
from contextlib import ExitStack

import numpy as np
import concourse.bass as bass
from concourse import mybir

P = 128
T, D = 256, 1024
NT = T // P
KC = D // P
H = 8
N_EXP, TOPK, FE = 32, 4, 1024
CAP = 64
ITEMS = N_EXP + (T * TOPK - N_EXP) // CAP + 1
ICOLS = ITEMS + 1
HG = 4
CB = 4
FF = 2816
FB = FF // P
UPG = FB // 2
LEVELS = (1, 2, 4, 8, 16, 32, 64)
ALPHA = 2.0 ** 0.25
LN_EPS, RMS_EPS = 1e-5, 1e-6
SWI_LIMIT, SWI_ALPHA = 7.0, 1.702
FAR = 16384.0
MASKED = -1e30
SLOT = 4096
SLOTS = 8
W2_SLOTS = 7
W2_FIRST = 6

_C = {}
_c = 0
for _name, _width in (("ident", P), ("flip", P), ("before", P), ("ones", P), ("slot", P), ("expert", N_EXP),
                      ("item", ICOLS), ("item64", ICOLS), ("strict", P), ("incl", P), ("quarter", 4 * CAP),
                      ("thresholds", 4), ("first", 1), ("index", 1)):
    _C[_name] = (_c, _c + _width)
    _c += _width
CONSTS = _c


def shape_constants():
    c = np.zeros((P, CONSTS), np.float32)
    p = np.arange(P)

    def put(name, value):
        c[:, _C[name][0]:_C[name][1]] = value

    put("ident", np.eye(P))
    put("flip", np.eye(P)[::-1])
    put("before", p[:, None] < p[None, :])
    put("ones", 1.0)
    put("slot", p[None, :] % CAP)
    put("expert", np.arange(N_EXP)[None, :])
    put("item", np.arange(ICOLS)[None, :])
    put("item64", CAP * np.arange(ICOLS)[None, :])
    put("strict", (p[:, None] < p[None, :] % N_EXP) & (p[:, None] < N_EXP))
    put("incl", (p[:, None] <= p[None, :] % N_EXP) & (p[:, None] < N_EXP))
    put("quarter", p[:, None] // N_EXP == np.arange(4 * CAP)[None, :] // CAP)
    put("thresholds", CAP * np.arange(4)[None, :])
    put("first", (p == 0)[:, None])
    put("index", p[:, None])
    levels = np.zeros((P, 1 + len(LEVELS), P), np.float32)
    levels[:, 0] = np.eye(P)
    for n, m in enumerate(LEVELS):
        same = p[:, None] // (2 * m) == p[None, :] // (2 * m)
        levels[:, n + 1] = same & (p[:, None] % (2 * m) < m) & (p[None, :] % (2 * m) >= m)
    dist = T - 1 - np.arange(2 * T)
    far = np.maximum(dist, 1).astype(np.float32)
    large = 16 + (np.log(far / 16) / np.float32(np.log(8.0)) * 16).astype(np.int32)
    bucket = np.where(dist < 16, dist, np.minimum(large, 31))
    buckets = ((np.arange(32)[:, None] == bucket[None, :]) & (dist >= 0)[None, :]).astype(np.float32)
    behind = np.broadcast_to(np.where(dist < 0, MASKED, 0.0), (H, 2 * T)).astype(np.float32)
    return c, levels, buckets, np.ascontiguousarray(behind)


def build(nc, x, rel_bias, a_w_in, a_w_out, ln_g, ln_b, w_router, b_router, w_gu, b_gu, w_down, b_down,
          w_in2, w_out2, conv_w, ffn_up, ffn_conv, ffn_down, hgrn_g, pre_mix_g, post_mix_g, pre_ffn_g,
          post_ffn_g, consts, levels, buckets, behind, rel_rows, out):
    f32, i32, u32 = mybir.dt.float32, mybir.dt.int32, mybir.dt.uint32
    ALU, ACT, AX = mybir.AluOpType, mybir.ActivationFunctionType, mybir.AxisListType

    with ExitStack() as ctx:
        def sb(name, shape, dt=f32):
            return ctx.enter_context(nc.sbuf_tensor(name, shape, dt))

        def sem(name):
            return ctx.enter_context(nc.semaphore(name))

        ring = sb("ring", [P, SLOTS * SLOT])
        cst = sb("cst", [P, CONSTS])
        vrow_a = sb("vrow_a", [P, P])
        vrow_b = sb("vrow_b", [36, P])
        vcol = sb("vcol", [P, 164])
        arena = sb("arena", [P, 18640])
        bank = [ctx.enter_context(nc.psum_tensor(f"bank{b}", [P, 512], f32)) for b in range(8)]

        def const(name, rows=P):
            return cst[0:rows, _C[name][0]:_C[name][1]]

        def at(start, *dims, rows=P):
            size = int(np.prod(dims))
            v = arena[0:rows, start:start + size]
            if len(dims) == 2:
                v = v.rearrange("p (a b) -> p a b", a=dims[0])
            if len(dims) == 3:
                v = v.rearrange("p (a b c) -> p a b c", a=dims[0], b=dims[1])
            return v

        def slot(s, a):
            return ring[:, s * SLOT:(s + 1) * SLOT].rearrange("p (a b) -> p a b", a=a)

        ident, ones = const("ident"), const("ones")

        roots = [(n, 1) for n in range(6)] + [(6, 2 * HG)] + [(n + 7, 1) for n in range(7, 13)]
        variance, inv_root, newton = at(18560, 24), at(18584, 24), at(18608, 24)

        x_tok = at(0, NT, D)
        xT = at(2048, KC, T)
        qT = at(4096, H, T)
        kT = at(6144, H, T)
        v_tok = at(8192, NT, D)
        bias = at(10240, H, 3 * P)
        prob = at(13312, 2, 3 * P)
        probT = at(14080, 2, 3 * P)
        oT = at(2048, H, T)
        neg_max = at(14848, H, 2)
        prob_sum = at(14864, H, 2)
        prob_inv = at(14880, H, 2)
        rel_tab = at(14912, 512, rows=H)
        bucket_sb = at(15424, 512, rows=32)
        behind_sb = at(15936, 512, rows=H)
        relb_sb = at(16448, H, rows=32)
        stats = at(16460, NT, 2, 6)
        moments = at(16484, NT, 2)
        row_g = at(16512, D)
        row_b = at(17536, D)

        h1 = at(4096, NT, D)
        h1T = at(2048, KC, T)
        xeT = at(6144, KC, CAP)
        bias_sel = at(6656, 4, CAP)
        sel = at(6912, NT, CAP)
        selg = at(7040, NT, P)
        selgT = at(7296, NT, P)
        hg = at(7552, 512)
        sig = at(8064, 512)
        hu = at(8576, 512)
        act_e = at(9088, 4, P)
        actT = at(9600, 4, P)
        y_item = at(10112, 512)
        bgu = at(10624, 512)
        bdown = at(11136, D, rows=N_EXP)
        wr = at(12160, KC, N_EXP)
        br = at(12416, N_EXP)
        logit = at(12448, NT, N_EXP)
        top8 = at(12512, NT, 8)
        top_i = at(12528, NT, 8).bitcast(u32)
        top_f = at(12544, NT, 8)
        gate_e = at(12560, NT, TOPK)
        gate_s = at(12568, NT)
        gate_r = at(12570, NT)
        gate = at(12572, NT, TOPK)
        hit = at(12580, NT, TOPK, N_EXP)
        chosen = at(12836, NT, N_EXP)
        gates = at(12900, NT, N_EXP)
        place = at(12964, NT, N_EXP)
        count = at(13028, 1, rows=N_EXP)
        over = at(13029, 4, rows=N_EXP)
        blocks = at(13033, 1, rows=N_EXP)
        span = at(13034, 2)
        span64 = at(13036, 1, rows=N_EXP)
        from_first = at(13037, ICOLS)
        owner = at(13096, ICOLS)
        gatesT = at(13200, T, rows=N_EXP)
        placeT = at(13456, T, rows=N_EXP)
        item_place = at(13712, NT, ICOLS)
        item_gate = at(13824, NT, ICOLS)
        item_exp = at(13936, ICOLS + 1, rows=1).bitcast(i32)

        x2 = at(0, NT, D)
        xn = at(2048, NT, D)
        gc = at(2048, CB, T)
        cm = at(3072, CB, T + 2)
        hT = at(4112, KC, T)
        q2 = at(6160, HG, T)
        lf = at(7184, HG, T)
        k2 = at(8208, HG, T)
        cum = at(9232, HG, T)
        cum2 = at(10256, HG, T)
        v2 = at(11280, NT, 512)
        sg2 = at(12304, NT, 512)
        zl = at(13328, HG, T)
        kl = at(14352, HG, T)
        ql = at(15376, HG, T)
        ss = at(16400, 16)
        s7 = (SLOTS - 1) * SLOT

        def scratch(start, *dims):
            size = int(np.prod(dims))
            v = ring[:, s7 + start:s7 + start + size]
            return v.rearrange("p (a b) -> p a b", a=dims[0]) if len(dims) == 2 else v

        att = scratch(0, 8, P)
        att2 = scratch(1024, HG, P)
        lev = scratch(1536, 1 + len(LEVELS), P)
        gb = scratch(2560, CB, T)
        o_tok = at(13328, NT, 512)
        mixT = at(4112, HG, T)
        x3 = at(6160, NT, D)
        aT = at(8208, FB, T)
        up_sb = at(13840, 2, 2 * (T + 2))
        cv = at(14872, 2, 2 * T)
        sgt = at(15896, 2, T)
        ss2 = at(16408, 16)
        sq_sum = at(16424, 16)
        y_out = at(2048, NT, D)

        x_in, const_in, rel_in, vrow_in = sem("x_in"), sem("const_in"), sem("rel_in"), sem("vrow_in")
        attn_w = [sem(f"attn_w{s}") for s in range(SLOTS)]
        moe_w = [sem(f"moe_w{s}") for s in range(6)]
        w2_in = [sem(f"w2_in{s}") for s in range(W2_SLOTS)]
        ln0_in, ln1_in, post_in = sem("ln0_in"), sem("ln1_in"), sem("post_in")
        rel_stored, bias_in = sem("rel_stored"), sem("bias_in")
        moe_small_in, lev_in = sem("moe_small_in"), sem("lev_in")
        rel_ps, rel_ready = sem("rel_ps"), sem("rel_ready")
        vcol_ps, vcol_ready = sem("vcol_ps"), sem("vcol_ready")
        xT_ps, xT_act, xT_dve = sem("xT_ps"), sem("xT_act"), sem("xT_dve")
        proj_ps, proj_act, proj_dve = sem("proj_ps"), sem("proj_act"), sem("proj_dve")
        s_ps, max_ready, exp_ready = sem("s_ps"), sem("max_ready"), sem("exp_ready")
        prob_ready, pt_ps, pt_ready, o_ps, o_ready = (sem("prob_ready"), sem("pt_ps"), sem("pt_ready"),
                                                      sem("o_ps"), sem("o_ready"))
        out_ps, h1_ready = sem("out_ps"), sem("h1_ready")
        h1T_ps, h1T_act, h1T_dve = sem("h1T_ps"), sem("h1T_act"), sem("h1T_dve")
        logit_ps, top_ready, gexp_ready = sem("logit_ps"), sem("top_ready"), sem("gexp_ready")
        route_ready, pos_ps, blocks_ready = sem("route_ready"), sem("pos_ps"), sem("blocks_ready")
        span_ps, owner_ready, items_ps, items_ready = (sem("span_ps"), sem("owner_ready"), sem("items_ps"),
                                                       sem("items_ready"))
        w_used = [sem(f"w_used{s}") for s in range(6)]
        gath_ps, xe_ready = sem("gath_ps"), sem("xe_ready")
        sel_ready, selg_ready, bsel_ready = sem("sel_ready"), sem("selg_ready"), sem("bsel_ready")
        hg_ready, gu_read, sig_ready, act_ready = (sem("hg_ready"), sem("gu_read"), sem("sig_ready"),
                                                   sem("act_ready"))
        actT_ps, actT_ready, selgT_ps, selgT_ready = (sem("actT_ps"), sem("actT_ready"), sem("selgT_ps"),
                                                      sem("selgT_ready"))
        y_ready, prod_ready, moe_done = sem("y_ready"), sem("prod_ready"), sem("moe_done")
        var_ready, rough_ready = sem("var_ready"), sem("rough_ready")
        x2_ready, xn_ready = sem("x2_ready"), sem("xn_ready")
        hT_ps, hT_act, hT_dve = sem("hT_ps"), sem("hT_act"), sem("hT_dve")
        f_abs, lf_ready, lfm_ready, k_ready = sem("f_abs"), sem("lf_ready"), sem("lfm_ready"), sem("k_ready")
        f_log = sem("f_log")
        q_sig, q_ready, g_sig, g_ready, v_ready = (sem("q_sig"), sem("q_ready"), sem("g_sig"), sem("g_ready"),
                                                   sem("v_ready"))
        gb_ready, gc_ready, ch_read, conv_ready = sem("gb_ready"), sem("gc_ready"), sem("ch_read"), sem("conv_ready")
        dec_ready, z_ready, ql_ready = sem("dec_ready"), sem("z_ready"), sem("ql_ready")
        lv_ps, lv_ready, o2_ps, o2_sq, o2_ready = (sem("lv_ps"), sem("lv_ready"), sem("o2_ps"), sem("o2_sq"),
                                                   sem("o2_ready"))
        mT_ps, mT_ready, mix_ps, mix_sq, x3_ready = (sem("mT_ps"), sem("mT_ready"), sem("mix_ps"), sem("mix_sq"),
                                                     sem("x3_ready"))
        x_sq, up_ps, up_ready, up_sig, a_ready = (sem("x_sq"), sem("up_ps"), sem("up_ready"), sem("up_sig"),
                                                  sem("a_ready"))
        cv_ready = sem("cv_ready")
        down_ps, down_sq, y_done, out_done = sem("down_ps"), sem("down_sq"), sem("y_done"), sem("out_done")
        dve_step, act_step = sem("dve_step"), sem("act_step")

        class Link:

            def __init__(self, eng, step):
                self.eng, self.step, self.n = eng, step, 0

            def __call__(self, ins):
                self.n += 1
                ins.then_inc(self.step, 1)
                self.eng.wait_ge(self.step, self.n)

        def row(v, n):
            return v.rearrange("(a n) -> a n", a=1).to_broadcast([P, n])

        w2_loads = []

        def w2_slot():
            return (W2_FIRST + len(w2_loads)) % W2_SLOTS

        for g in (1, 0, 2, 3, 4, 5, 6):
            s = w2_slot()
            w2_loads.append((s, [(slot(s, KC), w_in2[:, g * 512:(g + 1) * 512].rearrange("(c p) n -> p c n", p=P))]))
        for g in range(2):
            s = w2_slot()
            w2_loads.append((s, [(slot(s, KC), w_out2[:, g * 512:(g + 1) * 512].rearrange("(c p) n -> p c n", p=P))]))
        for g in range(UPG):
            s = w2_slot()
            w2_loads.append((s, [(slot(s, KC)[:, :, j * 256:(j + 1) * 256],
                                  ffn_up[:, j * FF + g * 256:j * FF + (g + 1) * 256].rearrange("(c p) n -> p c n", p=P))
                                 for j in range(2)]))
        for g in range(-(-FB // 4)):
            s = w2_slot()
            k = min(4, FB - 4 * g)
            w2_loads.append((s, [(slot(s, 4)[:, 0:k, :],
                                  ffn_down[g * 512:g * 512 + k * P, :].rearrange("(c p) n -> p c n", p=P))]))

        w2_count, seen = [], [0] * W2_SLOTS
        for s, parts in w2_loads:
            seen[s] += 16 * len(parts)
            w2_count.append(seen[s])

        block = ctx.enter_context(nc.Block())

        @block.sync
        def _(sp):
            sp.dma_start(x_tok, x.rearrange("(t p) d -> p t d", p=P)).then_inc(x_in, 16)
            sp.dma_start(cst[:, :], consts[:, :]).then_inc(const_in, 16)
            for s in range(6):
                sp.dma_start(slot(s, KC), a_w_in[:, s * 512:(s + 1) * 512].rearrange("(c p) n -> p c n", p=P)
                             ).then_inc(attn_w[s], 16)
            for g in range(2):
                sp.dma_start(slot(6 + g, KC), a_w_out[:, g * 512:(g + 1) * 512].rearrange("(c p) n -> p c n", p=P)
                             ).then_inc(attn_w[6 + g], 16)

            def load_expert(e, wait_slot):
                for s in range(6):
                    wait_slot(s)
                    if s < 4:
                        src = w_gu[bass.ds(e, 1), s * 256:(s + 1) * 256, :].rearrange("o (c p) n -> p (o c) n", p=P)
                        dst = slot(s, 2)
                    else:
                        src = w_down[bass.ds(e, 1), (s - 4) * 512:(s - 3) * 512, :].rearrange(
                            "o (c p) n -> p (o c) n", p=P)
                        dst = slot(s, 4)
                    sp.dma_start(dst, src).then_inc(moe_w[s], 16)

            load_expert(0, lambda s: sp.wait_ge(proj_ps, 2 * (s + 1)))
            sp.wait_ge(out_ps, 3)
            for dst, src in w2_loads[0][1]:
                sp.dma_start(dst, src).then_inc(w2_in[W2_FIRST], 16)
            sp.wait_ge(items_ready, 1)
            n_items = sp.value_load(item_exp[0:1, ICOLS:ICOLS + 1], min_val=1, max_val=ITEMS)
            with sp.Fori(1, ITEMS) as i:
                with sp.If(i < n_items):
                    e = sp.value_load(item_exp[0:1, bass.ds(i, 1)], min_val=0, max_val=N_EXP - 1)
                    load_expert(e, lambda s: sp.wait_ge(w_used[s], i))
            def wait_used(n):
                if n < 7:
                    sp.wait_ge(hT_ps, 4 + 2 * (n + 1))
                elif n < 9:
                    sp.wait_ge(mix_ps, n - 4)
                else:
                    sp.wait_ge(up_ps, 2 * (n - 9 + 1))

            sp.wait_ge(moe_done, 1)
            for n, (s, parts) in enumerate(w2_loads):
                if n == 0:
                    continue
                if n >= W2_SLOTS:
                    wait_used(n - W2_SLOTS)
                for dst, src in parts:
                    sp.dma_start(dst, src).then_inc(w2_in[s], 16)
            for t in range(NT):
                sp.wait_ge(y_done, t + 1)
                sp.dma_start(out[t * P:(t + 1) * P, :], y_out[:, t, :]).then_inc(out_done, 16)
            sp.wait_ge(out_done, 16 * NT)

        @block.gpsimd
        def _(pool):
            pool.dma_start(bucket_sb, buckets[:, :]).then_inc(rel_in, 16)
            pool.dma_start(behind_sb, behind[:, :]).then_inc(rel_in, 16)
            pool.dma_start(relb_sb, rel_bias[:, :]).then_inc(rel_in, 16)
            fc = ffn_conv.rearrange("j (f p) -> (j f) p", p=P)
            pool.dma_start(vrow_a[:, :], fc[0:P, :]).then_inc(vrow_in, 16)
            pool.dma_start(vrow_b[0:4, :], fc[P:132, :]).then_inc(vrow_in, 16)
            for start, rows, src in ((4, 8, pre_mix_g), (12, 8, pre_ffn_g)):
                pool.dma_start(vrow_b[start:start + rows, :], src.rearrange("(c p) -> c p", p=P)).then_inc(vrow_in, 16)
            pool.dma_start(vrow_b[20:32, :], conv_w.rearrange("j (c p) -> (j c) p", p=P)).then_inc(vrow_in, 16)
            pool.dma_start(vrow_b[32:36, :], hgrn_g.rearrange("(c p) -> c p", p=P)).then_inc(vrow_in, 16)
            pool.dma_start(row_g, row(ln_g[0, :], D)).then_inc(ln0_in, 16)
            pool.dma_start(row_b, row(ln_b[0, :], D)).then_inc(ln0_in, 16)
            pool.wait_ge(rel_ready, 1)
            pool.dma_start(rel_rows[:, :], rel_tab).then_inc(rel_stored, 16)
            pool.wait_ge(rel_stored, 16)
            rel_t = rel_rows.tensor
            pool.dma_start(bias[:, :, 0:P], bass.AP(rel_t, P, [[1, P], [2 * T, H], [1, P]])).then_inc(bias_in, 16)
            pool.dma_start(bias[:, :, P:3 * P], bass.AP(rel_t, 0, [[1, P], [2 * T, H], [1, 2 * P]])
                           ).then_inc(bias_in, 16)
            pool.wait_ge(prob_ready, H)
            pool.wait_ge(pt_ps, H)
            pool.dma_start(wr, w_router.rearrange("(c p) e -> p c e", p=P)).then_inc(moe_small_in, 16)
            pool.dma_start(br, row(b_router, N_EXP)).then_inc(moe_small_in, 16)
            for q in range(4):
                pool.dma_start(bgu[q * 32:(q + 1) * 32, :], b_gu[:, q * 512:(q + 1) * 512]).then_inc(moe_small_in, 16)
            pool.dma_start(bdown, b_down[:, :]).then_inc(moe_small_in, 16)
            pool.wait_ge(h1_ready, NT)
            pool.dma_start(row_g, row(ln_g[1, :], D)).then_inc(ln1_in, 16)
            pool.dma_start(row_b, row(ln_b[1, :], D)).then_inc(ln1_in, 16)
            pool.dma_start(lev, levels[:, :, :]).then_inc(lev_in, 16)
            pool.wait_ge(x2_ready, NT)
            pool.dma_start(row_g, row(post_mix_g, D)).then_inc(post_in, 16)
            pool.dma_start(row_b, row(post_ffn_g, D)).then_inc(post_in, 16)

        @block.tensor
        def _(pe):
            mm = pe.matmul

            def turn(dst, src, rows=P):
                return pe.transpose(dst, src, ident[0:rows, 0:rows])

            pe.wait_ge(const_in, 16)
            pe.wait_ge(x_in, 16)
            for t in range(NT):
                for g in range(2):
                    b = 2 * t + g
                    for j in range(4):
                        last = turn(bank[b][:, j * P:(j + 1) * P], x_tok[:, t, (4 * g + j) * P:(4 * g + j + 1) * P])
                    last.then_inc(xT_ps, 1)
            pe.wait_ge(xT_act, 2)
            pe.wait_ge(xT_dve, 2)
            for r in range(12):
                g, half = divmod(r, 2)
                b = (4 + r) % 8
                if half == 0:
                    pe.wait_ge(attn_w[g], 16)
                if r == 9:
                    pe.wait_ge(rel_in, 48)
                    pe.wait_ge(proj_act, 3)
                    mm(bank[0][0:H, :], relb_sb, bucket_sb, start=True, stop=True).then_inc(rel_ps, 1)
                    pe.wait_ge(vrow_in, 96)
                    pe.wait_ge(proj_dve, 3)
                    turn(bank[1][:, 0:P], vrow_a[:, :])
                    turn(bank[1][:, P:P + 36], vrow_b[:, :], 36).then_inc(vcol_ps, 1)
                if r >= 8:
                    pe.wait_ge(proj_dve if r % 2 else proj_act, (r - 8) // 2 + 1)
                w = slot(g, KC)
                if g < 4:
                    for j in range(2):
                        col = (2 * half + j) * P
                        for c in range(KC):
                            last = mm(bank[b][:, j * T:(j + 1) * T], w[:, c, col:col + P], xT[:, c, :],
                                      start=c == 0, stop=c == KC - 1)
                else:
                    for c in range(KC):
                        last = mm(bank[b][:, :], xT[:, c, half * P:(half + 1) * P], w[:, c, :],
                                  start=c == 0, stop=c == KC - 1)
                last.then_inc(proj_ps, 1)

            def scores(h):
                if h >= 2:
                    pe.wait_ge(exp_ready, h - 1)
                b = bank[h % 2]
                mm(b[:, 0:3 * P], const("flip"), bias[:, h, :], start=True, stop=True)
                mm(b[:, 0:P], qT[:, h, 0:P], kT[:, h, 0:P], start=False, stop=True, skip_group_check=True)
                mm(b[:, P:3 * P], qT[:, h, P:T], kT[:, h, :], start=False, stop=True,
                   skip_group_check=True).then_inc(s_ps, 1)

            def turn_probs(h):
                pe.wait_ge(prob_ready, h + 1)
                if h >= 2:
                    pe.wait_ge(pt_ready, h - 1)
                b, p = bank[2 + h % 2], prob[:, h % 2, :]
                for j in range(3):
                    last = turn(b[:, j * P:(j + 1) * P], p[:, j * P:(j + 1) * P])
                last.then_inc(pt_ps, 1)

            def values(h):
                pe.wait_ge(pt_ready, h + 1)
                if h >= 2:
                    pe.wait_ge(o_ready, h - 1)
                b, p = bank[4 + h % 2], probT[:, h % 2, :]
                mm(b[:, 0:T], v_tok[:, 0, h * P:(h + 1) * P], p[:, 0:T], start=True, stop=True)
                mm(b[:, P:T], v_tok[:, 1, h * P:(h + 1) * P], p[:, T:3 * P], start=False, stop=True,
                   skip_group_check=True).then_inc(o_ps, 1)

            pe.wait_ge(proj_act, 6)
            pe.wait_ge(proj_dve, 6)
            pe.wait_ge(bias_in, 32)
            pe.wait_ge(vcol_ready, 1)
            scores(0)
            scores(1)
            for h in range(H):
                turn_probs(h)
                if h + 2 < H:
                    scores(h + 2)
                values(h)
            pe.wait_ge(o_ready, H)
            for t in range(NT):
                for g in range(2):
                    pe.wait_ge(attn_w[6 + g], 16)
                    for h in range(H):
                        last = mm(bank[2 * g + t][:, :], oT[:, h, t * P:(t + 1) * P], slot(6 + g, KC)[:, h, :],
                                  start=h == 0, stop=h == H - 1)
                    last.then_inc(out_ps, 1)

            for t in range(NT):
                pe.wait_ge(h1_ready, t + 1)
                for g in range(2):
                    b = 4 + 2 * t + g
                    for j in range(4):
                        last = turn(bank[b][:, j * P:(j + 1) * P], h1[:, t, (4 * g + j) * P:(4 * g + j + 1) * P])
                    last.then_inc(h1T_ps, 1)
            pe.wait_ge(h1T_act, 2)
            pe.wait_ge(h1T_dve, 2)
            pe.wait_ge(moe_small_in, 7 * 16)
            for t in range(NT):
                for c in range(KC):
                    last = mm(bank[0][:, t * N_EXP:(t + 1) * N_EXP], h1T[:, c, t * P:(t + 1) * P], wr[:, c, :],
                              start=c == 0, stop=c == KC - 1)
            last.then_inc(logit_ps, 1)
            pe.wait_ge(route_ready, 1)
            before = const("before")
            mm(bank[1][:, 0:N_EXP], before, chosen[:, 0, :], start=True, stop=True)
            mm(bank[1][:, N_EXP:2 * N_EXP], ones, chosen[:, 0, :], start=True, stop=False)
            mm(bank[1][:, N_EXP:2 * N_EXP], before, chosen[:, 1, :], start=False, stop=True)
            for t in range(NT):
                mm(bank[2][0:N_EXP, 0:1], chosen[:, t, :], ones[:, 0:1], start=t == 0, stop=t == NT - 1)
            for t in range(NT):
                last = turn(bank[3][0:N_EXP, t * P:(t + 1) * P], gates[:, t, :])
            last.then_inc(pos_ps, 1)
            pe.wait_ge(blocks_ready, 1)
            mm(bank[0][:, 0:1], const("strict", N_EXP), blocks, start=True, stop=True)
            mm(bank[0][:, 1:2], const("incl", N_EXP), blocks, start=True, stop=True)
            for t in range(NT):
                last = turn(bank[1][0:N_EXP, t * P:(t + 1) * P], place[:, t, :])
            last.then_inc(span_ps, 1)
            pe.wait_ge(owner_ready, 1)
            own = owner[0:N_EXP, :]
            for t in range(NT):
                mm(bank[2][:, t * ICOLS:(t + 1) * ICOLS], placeT[:, t * P:(t + 1) * P], own, start=True, stop=True)
            for t in range(NT):
                mm(bank[3][:, t * ICOLS:(t + 1) * ICOLS], gatesT[:, t * P:(t + 1) * P], own, start=True, stop=True)
            mm(bank[0][0:1, 0:ICOLS], const("index", N_EXP), own, start=True, stop=True)
            mm(bank[0][0:1, ICOLS:ICOLS + 1], ones[0:N_EXP, 0:1], blocks, start=True, stop=True)
            for g in range(2):
                for t in range(NT):
                    last = mm(bank[4 + 2 * g + t][:, :], gatesT[:, t * P:(t + 1) * P], bdown[:, g * 512:(g + 1) * 512],
                              start=True, stop=True)
            last.then_inc(items_ps, 1)

            def gather():
                for c in range(KC):
                    for t in range(NT):
                        last = mm(bank[2][:, c * CAP:(c + 1) * CAP], h1[:, t, c * P:(c + 1) * P], sel[:, t, :],
                                  start=t == 0, stop=t == NT - 1)
                last.then_inc(gath_ps, 1)

            pe.wait_ge(sel_ready, 1)
            pe.wait_ge(items_ready, 1)
            gather()
            n_items = pe.value_load(item_exp[0:1, ICOLS:ICOLS + 1], min_val=1, max_val=ITEMS)
            with pe.Fori(0, ITEMS) as i:
                with pe.If(i < n_items):
                    pe.wait_ge(xe_ready, i + 1)
                    pe.wait_ge(bsel_ready, i + 1)
                    pe.wait_ge(gu_read, i + 1)
                    pe.wait_ge(y_ready, i + 1)
                    for q in range(4):
                        half = q % 2
                        mm(bank[q // 2][half * 64:half * 64 + 64, :], bias_sel[:, q, :], bgu, start=True, stop=False)
                    for c in range(KC):
                        if c % 2 == 0:
                            pe.wait_ge(moe_w[c // 2], i * 16 + 16)
                        w = slot(c // 2, 2)
                        for q in range(4):
                            half = q % 2
                            last = mm(bank[q // 2][half * 64:half * 64 + 64, :], xeT[:, c, :],
                                      w[:, c % 2, q * 512:(q + 1) * 512], start=False, stop=c == KC - 1)
                        if c % 2 == 1:
                            last.then_inc(w_used[c // 2], 1)
                    pe.wait_ge(sel_ready, i + 2)
                    pe.wait_ge(selgT_ready, i + 1)
                    gather()
                    pe.wait_ge(act_ready, i + 1)
                    for c in range(4):
                        last = turn(bank[3][:, c * P:(c + 1) * P], act_e[:, c, :])
                    last.then_inc(actT_ps, 1)
                    pe.wait_ge(selg_ready, i + 1)
                    pe.wait_ge(xe_ready, i + 2)
                    for t in range(NT):
                        last = turn(bank[2][:, t * P:(t + 1) * P], selg[:, t, :])
                    last.then_inc(selgT_ps, 1)
                    pe.wait_ge(actT_ready, i + 1)
                    for c in range(KC):
                        if c % 4 == 0:
                            pe.wait_ge(moe_w[4 + c // 4], i * 16 + 16)
                        lhs = actT[:, c % 4, (c // 4) * 64:(c // 4) * 64 + 64]
                        w = slot(4 + c // 4, 4)
                        for half in range(2):
                            last = mm(bank[1][half * 64:half * 64 + 64, :], lhs,
                                      w[:, c % 4, half * 512:(half + 1) * 512], start=c == 0, stop=c == KC - 1)
                        if c % 4 == 3:
                            last.then_inc(w_used[4 + c // 4], 1)
                    pe.wait_ge(y_ready, i + 2)
                    pe.wait_ge(selgT_ready, i + 2)
                    for t in range(NT):
                        for half in range(2):
                            rows = slice(half * 64, half * 64 + 64)
                            mm(bank[4 + 2 * half + t][:, :], selgT[rows, t, :], y_item[rows, :],
                               start=False, stop=True, skip_group_check=True)
            pe.drain().then_inc(moe_done, 1)

            def turn_tokens(src, ready, ps):
                for t in range(NT):
                    pe.wait_ge(*ready(t))
                for b in range(4):
                    for j in range(2):
                        for t in range(NT):
                            last = turn(bank[b][:, j * T + t * P:j * T + (t + 1) * P],
                                        src[:, t, (2 * b + j) * P:(2 * b + j + 1) * P])
                    last.then_inc(ps, 1)

            def w2_wait(n):
                pe.wait_ge(w2_in[w2_loads[n][0]], w2_count[n])
                return slot(w2_loads[n][0], KC)

            def channels(w, dst, col):
                for c in range(KC):
                    last = mm(dst, w[:, c, col:col + P], hT[:, c, :], start=c == 0, stop=c == KC - 1)
                return last

            turn_tokens(xn, lambda t: (xn_ready, t + 1), hT_ps)
            pe.wait_ge(hT_act, 4)
            pe.wait_ge(hT_dve, 4)
            for n in range(4):
                w = w2_wait(n)
                for half in range(2):
                    b = bank[2 * n + half]
                    if n >= 2:
                        for c in range(KC):
                            last = mm(b[:, :], hT[:, c, half * P:(half + 1) * P], w[:, c, :],
                                      start=c == 0, stop=c == KC - 1)
                    else:
                        for j in range(2):
                            last = channels(w, b[:, j * T:(j + 1) * T], (2 * half + j) * P)
                    last.then_inc(hT_ps, 1)

            def level(n):
                if n == 0:
                    pe.wait_ge(k_ready, 2)
                    pe.wait_ge(q_ready, 2)
                    pe.wait_ge(g_ready, 2)
                else:
                    pe.wait_ge(ql_ready, n)
                    pe.wait_ge(lv_ready, n)
                ks, qs = (k2, q2) if n == 0 else (kl, ql)
                for b in range(2):
                    for j in range(4):
                        h, t = 2 * b + j // 2, j % 2
                        last = mm(bank[6 + b][:, j * P:(j + 1) * P], ks[:, h, t * P:(t + 1) * P],
                                  qs[:, h, t * P:(t + 1) * P], start=True, stop=True)
                    last.then_inc(lv_ps, 1)

            done = 0
            for n in range(4, 7):
                w = w2_wait(n)
                pe.wait_ge(*((lfm_ready, 2), (q_ready, 2), (v_ready, 2))[n - 4])
                for half in range(2):
                    for j in range(2):
                        last = channels(w, bank[2 * (n - 4) + half][:, j * T:(j + 1) * T], (2 * half + j) * P)
                        if j == 1:
                            last.then_inc(hT_ps, 1)
                        if 4 * (n - 4) + 2 * half + j >= 3 and done <= len(LEVELS):
                            level(done)
                            done += 1
            assert done == 1 + len(LEVELS)
            pe.wait_ge(ql_ready, len(LEVELS) + 1)
            pe.wait_ge(gc_ready, 2)
            for h in range(HG):
                last = mm(bank[2][:, h * P:(h + 1) * P], kl[:, h, 0:P], ql[:, h, P:T], start=True, stop=True)
            last.then_inc(lv_ps, 1)
            pe.wait_ge(lv_ready, len(LEVELS) + 2)
            pe.wait_ge(gb_ready, 2)
            pe.wait_ge(v_ready, 2)
            for h in range(HG):
                mm(bank[0][:, h * P:(h + 1) * P], att[:, 2 * h, :], v2[:, 0, h * P:(h + 1) * P], start=True, stop=True)
                mm(bank[1][:, h * P:(h + 1) * P], att[:, 2 * h + 1, :], v2[:, 1, h * P:(h + 1) * P],
                   start=True, stop=False)
                last = mm(bank[1][:, h * P:(h + 1) * P], att2[:, h, :], v2[:, 0, h * P:(h + 1) * P],
                          start=False, stop=True)
            last.then_inc(o2_ps, 1)
            def mix(t, g, chunks):
                w = slot(w2_loads[7 + g][0], KC)
                for c in chunks:
                    lhs = mixT[:, c, t * P:(t + 1) * P] if c < HG else gb[:, c - HG, t * P:(t + 1) * P]
                    last = mm(bank[2 + 2 * t + g][:, :], lhs, w[:, c, :], start=c == HG, stop=c == HG - 1)
                return last

            pe.wait_ge(conv_ready, CB)
            for g in range(2):
                w2_wait(7 + g)
                for t in range(NT):
                    mix(t, g, range(HG, KC))
            pe.wait_ge(o2_ready, 1)
            for g in range(2):
                for j in range(2):
                    for t in range(NT):
                        h = 2 * g + j
                        last = turn(bank[6 + g][:, j * T + t * P:j * T + (t + 1) * P],
                                    o_tok[:, t, h * P:(h + 1) * P])
                last.then_inc(mT_ps, 1)
            pe.wait_ge(mT_ready, 4)
            for t in range(NT):
                for g in range(2):
                    mix(t, g, range(HG)).then_inc(mix_ps, 1)
            pe.wait_ge(x3_ready, NT)
            turn_tokens(xn, lambda t: (xn_ready, NT + t + 1), hT_ps)
            pe.wait_ge(hT_act, 8)
            pe.wait_ge(hT_dve, 8)
            for g in range(UPG):
                w = w2_wait(9 + g)
                for j in range(2):
                    f = 2 * g + j
                    if f >= 2:
                        pe.wait_ge(up_ready, f - 1)
                    b = bank[4 + f % 2]
                    channels(w, b[:, 0:T], j * P)
                    channels(w, b[:, T:2 * T], 256 + j * P).then_inc(up_ps, 1)
            def down(c, t):
                w = slot(w2_loads[9 + UPG + c // 4][0], 4)
                for g in range(2):
                    last = mm(bank[2 * t + g][:, :], aT[:, c, t * P:(t + 1) * P],
                              w[:, c % 4, g * 512:(g + 1) * 512], start=c == 0, stop=c == FB - 1)
                return last

            tail = FB - 4
            for c in range(tail):
                if c % 4 == 0:
                    w2_wait(9 + UPG + c // 4)
                pe.wait_ge(a_ready, c + 1)
                for t in range(NT):
                    down(c, t)
            w2_wait(9 + UPG + FB // 4)
            pe.wait_ge(a_ready, FB)
            for t in range(NT):
                for c in range(tail, FB):
                    last = down(c, t)
                last.then_inc(down_ps, 1)

        @block.scalar
        def _(act):
            link = Link(act, act_step)
            copy = nc.scalar.copy
            activate = nc.scalar.activation

            def rough_root(n):
                c, k = roots[n]
                act.wait_ge(var_ready, n + 1)
                link(activate(inv_root[:, c:c + k], variance[:, c:c + k], ACT.Ln))
                activate(inv_root[:, c:c + k], inv_root[:, c:c + k], ACT.Exp, scale=-0.5).then_inc(rough_ready, 1)

            for b in (0, 2):
                act.wait_ge(xT_ps, b + 1)
                copy(xT[:, 0:4, (b // 2) * P:(b // 2 + 1) * P],
                     bank[b][:, :].rearrange("p (c n) -> p c n", c=4)).then_inc(xT_act, 1)
            for r in range(0, 12, 2):
                act.wait_ge(proj_ps, r + 1)
                src = bank[(4 + r) % 8][:, :]
                if r < 8:
                    dst, h = (qT, r) if r < 4 else (kT, r - 4)
                    scale = float(P) ** -0.5 if r < 4 else 1.0
                    activate(dst[:, 2 * h:2 * h + 2, :], src.rearrange("p (c n) -> p c n", c=2), ACT.Copy,
                             scale=scale).then_inc(proj_act, 1)
                else:
                    copy(v_tok[:, 0, (r - 8) // 2 * 512:((r - 8) // 2 + 1) * 512], src).then_inc(proj_act, 1)
            for h in range(H + 1):
                if h < H:
                    act.wait_ge(max_ready, h + 1)
                    if h >= 2:
                        act.wait_ge(pt_ps, h - 1)
                    p, s = prob[:, h % 2, :], bank[h % 2]
                    activate(p[:, 0:P], s[:, 0:P], ACT.Exp, bias=neg_max[:, h, 0:1], accum_out=prob_sum[:, h, 0:1])
                    activate(p[:, P:3 * P], s[:, P:3 * P], ACT.Exp, bias=neg_max[:, h, 1:2],
                             accum_out=prob_sum[:, h, 1:2]).then_inc(exp_ready, 1)
                if h >= 1:
                    g = h - 1
                    act.wait_ge(pt_ps, g + 1)
                    if g >= 2:
                        act.wait_ge(o_ps, g - 1)
                    copy(probT[:, g % 2, :], bank[2 + g % 2][:, 0:3 * P]).then_inc(pt_ready, 1)
                    act.wait_ge(o_ps, g + 1)
                    copy(oT[:, g, :], bank[4 + g % 2][:, 0:T]).then_inc(o_ready, 1)
            rough_root(0)
            rough_root(1)
            for b in (4, 6):
                act.wait_ge(h1T_ps, b - 3)
                copy(h1T[:, 0:4, (b // 2 - 2) * P:(b // 2 - 1) * P],
                     bank[b][:, :].rearrange("p (c n) -> p c n", c=4)).then_inc(h1T_act, 1)
            act.wait_ge(top_ready, 1)
            for t in range(NT):
                last = activate(gate_e[:, t, :], top8[:, t, 0:TOPK], ACT.Exp, bias=gate_s[:, t:t + 1],
                                accum_out=gate_r[:, t:t + 1])
            last.then_inc(gexp_ready, 1)

            def take_tokens():
                copy(xeT.rearrange("p c n -> p (c n)"), bank[2][:, :]).then_inc(xe_ready, 1)

            act.sem_inc(y_ready, 1)
            act.sem_inc(selgT_ready, 1)
            act.wait_ge(gath_ps, 1)
            take_tokens()
            act.wait_ge(items_ready, 1)
            n_items = act.value_load(item_exp[0:1, ICOLS:ICOLS + 1], min_val=1, max_val=ITEMS)
            with act.Fori(0, ITEMS) as i:
                with act.If(i < n_items):
                    act.wait_ge(hg_ready, i + 1)
                    activate(sig, hg, ACT.Sigmoid, scale=SWI_ALPHA).then_inc(sig_ready, 1)
                    act.wait_ge(gath_ps, i + 2)
                    take_tokens()
                    act.wait_ge(actT_ps, i + 1)
                    copy(actT.rearrange("p c n -> p (c n)"), bank[3][:, :]).then_inc(actT_ready, 1)
                    act.wait_ge(selgT_ps, i + 1)
                    copy(selgT.rearrange("p c n -> p (c n)"), bank[2][:, 0:T]).then_inc(selgT_ready, 1)
                    act.wait_ge(w_used[5], i + 1)
                    copy(y_item, bank[1][:, :]).then_inc(y_ready, 1)

            def unused(start, size):
                return at(14352 + start, size)

            rough_root(2)
            rough_root(3)
            for t in range(NT):
                act.wait_ge(x2_ready, t + 1)
                activate(unused(t * D, D), x2[:, t, :], ACT.Square, accum_out=ss[:, t:t + 1]).then_inc(x_sq, 1)
            rough_root(4)
            rough_root(5)
            for b in (0, 2):
                act.wait_ge(hT_ps, b + 1)
                for j in range(2):
                    c = 2 * b + j
                    activate(hT[:, c, :], bank[b][:, j * T:(j + 1) * T], ACT.Copy,
                             scale=vcol[:, 132 + c:133 + c]).then_inc(hT_act, 1)
            for b in range(2):
                act.wait_ge(hT_ps, 4 + b + 1)
                z = zl[:, 2 * b:2 * b + 2, :].rearrange("p c n -> p (c n)")
                activate(z, bank[b][:, :], ACT.Abs).then_inc(f_abs, 1)
                act.wait_ge(f_abs, b + 1)
                link(activate(z, z, ACT.Exp, scale=-1.0))
                activate(z, z, ACT.Ln, bias=1.0).then_inc(f_log, 1)
            for b in range(2):
                act.wait_ge(lfm_ready, b + 1)
                z = k2[:, 2 * b:2 * b + 2, :]
                activate(z, z, ACT.Exp).then_inc(k_ready, 1)
            for b in range(2):
                act.wait_ge(hT_ps, 6 + b + 1)
                activate(kl[:, 2 * b:2 * b + 2, :].rearrange("p c n -> p (c n)"), bank[2 + b][:, :], ACT.Sigmoid
                         ).then_inc(q_sig, 1)
            for t in range(NT):
                act.wait_ge(hT_ps, 8 + t + 1)
                copy(v2[:, t, :], bank[4 + t][:, :]).then_inc(v_ready, 1)
            for t in range(NT):
                act.wait_ge(hT_ps, 10 + t + 1)
                activate(sg2[:, t, :], bank[6 + t][:, :], ACT.Sigmoid).then_inc(g_sig, 1)

            def decay(n):
                act.wait_ge(dec_ready, n + 1)
                activate(zl, zl, ACT.Exp).then_inc(z_ready, 1)

            def take(ps, banks, dst, done):
                for b in range(2):
                    act.wait_ge(hT_ps, ps + b + 1)
                    copy(dst[:, 2 * b:2 * b + 2, :].rearrange("p c n -> p (c n)"), bank[banks + b][:, :]
                         ).then_inc(done, 1)

            decay(0)
            take(12, 0, gb, gb_ready)
            decay(1)
            decay(2)
            take(14, 2, gc, gc_ready)
            for n in range(3, len(LEVELS) + 1):
                decay(n)
            act.wait_ge(o2_ps, 1)
            for t in range(NT):
                for h in range(HG):
                    last = activate(unused((t * HG + h) * P, P), bank[t][:, h * P:(h + 1) * P], ACT.Square,
                                    accum_out=ss[:, 2 + t * HG + h:3 + t * HG + h])
            last.then_inc(o2_sq, 1)
            rough_root(6)
            for g in range(2):
                act.wait_ge(mT_ps, g + 1)
                for j in range(2):
                    h = 2 * g + j
                    activate(mixT[:, h, :], bank[6 + g][:, j * T:(j + 1) * T], ACT.Copy,
                             scale=vcol[:, 160 + h:161 + h]).then_inc(mT_ready, 1)

            def squares_of(ps, count, banks, done):
                for n, b in enumerate(banks):
                    if n % count == 0:
                        act.wait_ge(ps[0], ps[1](n))
                    last = activate(unused(n * 512, 512), bank[b][:, :], ACT.Square, accum_out=ss2[:, n:n + 1])
                    last.then_inc(done, 1)

            squares_of((mix_ps, lambda n: n + 2), 2, (2, 3, 4, 5), mix_sq)
            rough_root(7)
            rough_root(8)
            for t in range(NT):
                act.wait_ge(x3_ready, t + 1)
                activate(unused(t * D, D), x3[:, t, :], ACT.Square, accum_out=ss2[:, 4 + t:5 + t]).then_inc(x_sq, 1)
            rough_root(9)
            rough_root(10)
            for b in (0, 2):
                act.wait_ge(hT_ps, 18 + b + 1)
                for j in range(2):
                    c = 2 * b + j
                    activate(hT[:, c, :], bank[b][:, j * T:(j + 1) * T], ACT.Copy,
                             scale=vcol[:, 140 + c:141 + c]).then_inc(hT_act, 1)

            def sigmoid_gate(f):
                act.wait_ge(cv_ready, f + 1)
                activate(sgt[:, f % 2, :], cv[:, f % 2, 0:T], ACT.Sigmoid).then_inc(up_sig, 1)

            for f in range(FB):
                act.wait_ge(up_ps, f + 1)
                if f >= 2:
                    act.wait_ge(a_ready, f - 1)
                u = up_sb[:, f % 2, :].rearrange("p (g n) -> p g n", g=2)
                copy(u[:, :, 2:T + 2], bank[4 + f % 2][:, :].rearrange("p (g n) -> p g n", g=2)
                     ).then_inc(up_ready, 1)
                if f >= 1:
                    sigmoid_gate(f - 1)
            sigmoid_gate(FB - 1)
            act.wait_ge(down_ps, 1)
            squares_of((down_ps, lambda n: n // 2 + 1), 2, (0, 1, 2, 3), down_sq)
            rough_root(11)
            rough_root(12)

        @block.vector
        def _(dve):
            link = Link(dve, dve_step)
            tt, ts, stt = dve.tensor_tensor, dve.tensor_scalar, dve.scalar_tensor_tensor
            for b in (1, 3):
                dve.wait_ge(xT_ps, b + 1)
                dve.tensor_copy(xT[:, 4:8, (b // 2) * P:(b // 2 + 1) * P],
                                bank[b][:, :].rearrange("p (c n) -> p c n", c=4)).then_inc(xT_dve, 1)
            for r in range(1, 12, 2):
                if r == 9:
                    dve.wait_ge(rel_ps, 1)
                    tt(rel_tab, bank[0][0:H, :], behind_sb, ALU.add).then_inc(rel_ready, 1)
                    dve.wait_ge(vcol_ps, 1)
                    dve.tensor_copy(vcol[:, :], bank[1][:, 0:164]).then_inc(vcol_ready, 1)
                dve.wait_ge(proj_ps, r + 1)
                src = bank[(4 + r) % 8][:, :]
                if r < 8:
                    dst, h = (qT, r) if r < 4 else (kT, r - 4)
                    scale = float(P) ** -0.5 if r < 4 else 1.0
                    ts(dst[:, 2 * h:2 * h + 2, :], src.rearrange("p (c n) -> p c n", c=2), scale, None, ALU.mult
                       ).then_inc(proj_dve, 1)
                else:
                    dve.tensor_copy(v_tok[:, 1, (r - 9) // 2 * 512:((r - 9) // 2 + 1) * 512], src
                                    ).then_inc(proj_dve, 1)

            def row_max(h):
                dve.wait_ge(s_ps, h + 1)
                p = bank[h % 2]
                dve.tensor_reduce(neg_max[:, h, 0:1], p[:, 0:P], AX.X, ALU.max, negate=True)
                dve.tensor_reduce(neg_max[:, h, 1:2], p[:, P:3 * P], AX.X, ALU.max, negate=True
                                  ).then_inc(max_ready, 1)

            def normalise(h):
                dve.wait_ge(exp_ready, h + 1)
                p = prob[:, h % 2, :]
                link(dve.reciprocal(prob_inv[:, h, :], prob_sum[:, h, :]))
                ts(p[:, 0:P], p[:, 0:P], prob_inv[:, h, 0:1], None, ALU.mult)
                ts(p[:, P:3 * P], p[:, P:3 * P], prob_inv[:, h, 1:2], None, ALU.mult).then_inc(prob_ready, 1)

            row_max(0)
            for h in range(H):
                if h + 1 < H:
                    row_max(h + 1)
                normalise(h)

            def root_of(n, src, scale, eps):
                c, k = roots[n]
                ts(variance[:, c:c + k], src, scale, eps, ALU.mult, ALU.add).then_inc(var_ready, 1)

            def refine(n):
                c, k = roots[n]
                v, y, w = (a[:, c:c + k] for a in (variance, inv_root, newton))
                dve.wait_ge(rough_ready, n + 1)
                link(tt(w, y, y, ALU.mult))
                link(tt(w, w, v, ALU.mult))
                link(ts(w, w, -0.5, 1.5, ALU.mult, ALU.add))
                link(tt(y, y, w, ALU.mult))
                return y

            def root(n, src, scale, eps):
                root_of(n, src, scale, eps)
                return refine(n)

            def layer_norm(z, base, banks, n, done, ready):
                def moments_of(t):
                    dve.wait_ge(*done(t))
                    for g in range(2):
                        cols = slice(g * 512, (g + 1) * 512)
                        last = stt(z[:, t, cols], base[:, t, cols], ALPHA, banks[2 * g + t][:, :], ALU.mult, ALU.add)
                    link(last)
                    for g in range(2):
                        last = dve.bn_stats(stats[:, t, g, :], z[:, t, g * 512:(g + 1) * 512])
                    link(last)
                    link(dve.bn_aggr(moments[:, t, :], stats[:, t, :, :].rearrange("p a b -> p (a b)")))
                    root_of(n + t, moments[:, t, 1:2], 1.0, LN_EPS)

                def scale(t):
                    r = refine(n + t)
                    link(stt(z[:, t, :], z[:, t, :], moments[:, t, 0:1], row_g, ALU.subtract, ALU.mult))
                    stt(z[:, t, :], z[:, t, :], r, row_b, ALU.mult, ALU.add).then_inc(ready, 1)

                moments_of(0)
                moments_of(1)
                scale(0)
                scale(1)

            dve.wait_ge(ln0_in, 32)
            layer_norm(h1, x_tok, bank[0:4], 0, lambda t: (out_ps, 2 * t + 2), h1_ready)
            for b in (5, 7):
                dve.wait_ge(h1T_ps, b - 3)
                dve.tensor_copy(h1T[:, 4:8, (b // 2 - 2) * P:(b // 2 - 1) * P],
                                bank[b][:, :].rearrange("p (c n) -> p c n", c=4)).then_inc(h1T_dve, 1)

            dve.wait_ge(logit_ps, 1)
            for t in range(NT):
                last = tt(logit[:, t, :], bank[0][:, t * N_EXP:(t + 1) * N_EXP], br, ALU.add)
            link(last)
            for t in range(NT):
                last = dve.max(top8[:, t, :], logit[:, t, :])
            link(last)
            ts(gate_s, top8[:, :, 0], -1.0, None, ALU.mult).then_inc(top_ready, 1)
            for t in range(NT):
                last = dve.max_index(top_i[:, t, :], top8[:, t, :], logit[:, t, :])
            link(last)
            link(dve.tensor_copy(top_f, top_i))
            for t in range(NT):
                for k in range(TOPK):
                    last = ts(hit[:, t, k, :], const("expert"), top_f[:, t, k:k + 1], None, ALU.is_equal)
            link(last)
            link(dve.tensor_reduce(chosen, hit.rearrange("p t k e -> p t e k"), AX.X, ALU.add))
            dve.wait_ge(gexp_ready, 1)
            link(dve.reciprocal(gate_r, gate_r))
            for t in range(NT):
                last = ts(gate[:, t, :], gate_e[:, t, :], gate_r[:, t:t + 1], None, ALU.mult)
            link(last)
            for t in range(NT):
                last = ts(gates[:, t, :], hit[:, t, 0, :], gate[:, t, 0:1], None, ALU.mult)
            link(last)
            for k in range(1, TOPK):
                for t in range(NT):
                    last = stt(gates[:, t, :], hit[:, t, k, :], gate[:, t, k:k + 1], gates[:, t, :],
                               ALU.mult, ALU.add)
                if k < TOPK - 1:
                    link(last)
            last.then_inc(route_ready, 1)

            dve.wait_ge(pos_ps, 1)
            link(dve.tensor_copy(count, bank[2][0:N_EXP, 0:1]))
            link(ts(over, const("thresholds", N_EXP), count[:, 0:1], None, ALU.is_lt))
            link(dve.tensor_reduce(blocks, over, AX.X, ALU.add))
            link(stt(place.rearrange("p t e -> p (t e)"), bank[1][:, 0:2 * N_EXP], FAR,
                     chosen.rearrange("p t e -> p (t e)"), ALU.add, ALU.mult))
            link(ts(place, place, -FAR, None, ALU.add))
            link(dve.tensor_copy(gatesT, bank[3][0:N_EXP, 0:T]))
            tt(blocks, blocks, const("first", N_EXP), ALU.max).then_inc(blocks_ready, 1)
            dve.wait_ge(span_ps, 1)
            link(dve.tensor_copy(span, bank[0][:, 0:2]))
            link(ts(from_first, const("item"), span[:, 0:1], None, ALU.is_ge))
            link(ts(span64, span[0:N_EXP, 0:1], float(CAP), None, ALU.mult))
            link(ts(placeT, bank[1][0:N_EXP, 0:T], span64[:, 0:1], None, ALU.add))
            stt(owner, const("item"), span[:, 1:2], from_first, ALU.is_lt, ALU.mult).then_inc(owner_ready, 1)
            dve.wait_ge(items_ps, 1)
            for t in range(NT):
                tt(item_place[:, t, :], bank[2][:, t * ICOLS:(t + 1) * ICOLS], const("item64"), ALU.subtract)
            link(dve.tensor_copy(item_gate.rearrange("p t i -> p (t i)"), bank[3][:, 0:NT * ICOLS]))
            dve.tensor_copy(item_exp, bank[0][0:1, 0:ICOLS + 1]).then_inc(items_ready, 1)
            dve.wait_ge(items_ready, 1)

            places = const("slot")

            def select(i):
                for t in range(NT):
                    last = ts(sel[:, t, :], places[:, 0:CAP], item_place[:, t, bass.ds(i, 1)], None, ALU.is_equal)
                last.then_inc(sel_ready, 1)

            def select_bias(i):
                ts(bias_sel.rearrange("p q n -> p (q n)"), const("quarter"), owner[:, bass.ds(i, 1)], None,
                   ALU.mult).then_inc(bsel_ready, 1)

            select(0)
            select_bias(0)
            dve.sem_inc(gu_read, 1)
            n_items = dve.value_load(item_exp[0:1, ICOLS:ICOLS + 1], min_val=1, max_val=ITEMS)
            with dve.Fori(0, ITEMS) as i:
                with dve.If(i < n_items):
                    dve.wait_ge(gath_ps, i + 1)
                    select(i + 1)
                    dve.wait_ge(selgT_ready, i + 1)
                    for t in range(NT):
                        last = ts(selg[:, t, :], places, item_place[:, t, bass.ds(i, 1)],
                                  item_gate[:, t, bass.ds(i, 1)], ALU.is_equal, ALU.mult)
                    last.then_inc(selg_ready, 1)
                    dve.wait_ge(w_used[3], i + 1)
                    ts(hg, bank[0][:, :], SWI_LIMIT, None, ALU.min).then_inc(hg_ready, 1)
                    ts(hu, bank[1][:, :], SWI_LIMIT, -SWI_LIMIT, ALU.min, ALU.max).then_inc(gu_read, 1)
                    select_bias(i + 1)
                    dve.wait_ge(gu_read, i + 2)
                    stt(hu, hu, 1.0, hg, ALU.add, ALU.mult).then_inc(prod_ready, 1)
                    dve.wait_ge(prod_ready, i + 1)
                    dve.wait_ge(sig_ready, i + 1)
                    tt(act_e.rearrange("p c n -> p (c n)"), hu, sig, ALU.mult).then_inc(act_ready, 1)

            dve.wait_ge(moe_done, 1)
            dve.wait_ge(ln1_in, 32)
            layer_norm(x2, h1, bank[4:8], 2, lambda t: (moe_done, 1), x2_ready)

            for t in range(NT):
                dve.wait_ge(x_sq, t + 1)
                r = root(4 + t, ss[:, t:t + 1], 1.0 / D, RMS_EPS)
                ts(xn[:, t, :], x2[:, t, :], r, None, ALU.mult).then_inc(xn_ready, 1)
            for b in (1, 3):
                dve.wait_ge(hT_ps, b + 1)
                for j in range(2):
                    c = 2 * b + j
                    ts(hT[:, c, :], bank[b][:, j * T:(j + 1) * T], vcol[:, 132 + c:133 + c], None, ALU.mult
                       ).then_inc(hT_dve, 1)
            marks = ql.rearrange("p h t -> p (h t)")
            link(dve.memset(marks, 1.0))
            link(dve.memset(marks[:, 0:HG * T:64], 0.0))
            link(dve.memset(att, 0.0))
            for b in range(2):
                dve.wait_ge(f_log, b + 1)
                cols = slice(2 * b, 2 * b + 2)
                dst = lf[:, cols, :].rearrange("p c n -> p (c n)")
                link(stt(dst, bank[b][:, :], 0.0, zl[:, cols, :].rearrange("p c n -> p (c n)"),
                         ALU.min, ALU.subtract))
                tt(k2[:, cols, :].rearrange("p c n -> p (c n)"), dst, bank[b][:, :], ALU.subtract
                   ).then_inc(lfm_ready, 1)
            flat = lf.rearrange("p h t -> p (h t)")
            link(dve.tensor_tensor_scan(cum.rearrange("p h t -> p (h t)"), marks, flat, 0.0, ALU.mult, ALU.add))
            link(dve.memset(marks[:, 64:HG * T:128], 1.0))
            link(dve.tensor_tensor_scan(cum2.rearrange("p h t -> p (h t)"), marks, flat, 0.0, ALU.mult, ALU.add))

            def squares(buffer, n):
                return buffer.rearrange("p h t -> p (h t)").rearrange("p (a b) -> p a b", b=2 * LEVELS[n])

            def decays(n):
                src, dst = squares(cum if LEVELS[n] < 64 else cum2, n), squares(zl, n)
                m = LEVELS[n]
                mid = src[:, :, m - 1:m].to_broadcast([P, HG * T // (2 * m), m])
                tt(dst[:, :, 0:m], mid, src[:, :, 0:m], ALU.subtract)
                tt(dst[:, :, m:2 * m], src[:, :, m:2 * m], mid, ALU.subtract).then_inc(dec_ready, 1)

            decays(0)
            for b in range(2):
                dve.wait_ge(q_sig, b + 1)
                cols = slice(2 * b, 2 * b + 2)
                stt(q2[:, cols, :].rearrange("p c n -> p (c n)"), bank[2 + b][:, :], float(P) ** -0.5,
                    kl[:, cols, :].rearrange("p c n -> p (c n)"), ALU.mult, ALU.mult).then_inc(q_ready, 1)
            for t in range(NT):
                dve.wait_ge(g_sig, t + 1)
                tt(sg2[:, t, :], sg2[:, t, :], bank[6 + t][:, :], ALU.mult).then_inc(g_ready, 1)
            dve.wait_ge(q_ready, 2)
            dve.wait_ge(lev_in, 16)

            def keep(n):
                for b in range(2):
                    dve.wait_ge(lv_ps, 2 * n + b + 1)
                    mask = lev[:, n:n + 1, :].to_broadcast([P, 4, P]).bitcast(u32)
                    last = dve.copy_predicated(att[:, 4 * b:4 * b + 4, :], mask,
                                               bank[6 + b][:, :].rearrange("p (a n) -> p a n", a=4))
                last.then_inc(lv_ready, 1)

            def decayed(n):
                m = LEVELS[n]
                dve.wait_ge(z_ready, n + 1)
                tt(squares(kl, n)[:, :, 0:m], squares(k2, n)[:, :, 0:m], squares(zl, n)[:, :, 0:m], ALU.mult)
                tt(squares(ql, n)[:, :, m:2 * m], squares(q2, n)[:, :, m:2 * m], squares(zl, n)[:, :, m:2 * m],
                   ALU.mult).then_inc(ql_ready, 1)
                dve.wait_ge(ql_ready, n + 1)

            for n in range(len(LEVELS)):
                if n:
                    dve.wait_ge(lv_ps, 2 * n + 2)
                decayed(n)
                if n + 1 < len(LEVELS):
                    decays(n + 1)
                else:
                    link(tt(zl[:, :, 0:P], cum2[:, :, P - 1:P].to_broadcast([P, HG, P]), cum2[:, :, 0:P],
                            ALU.subtract))
                    dve.tensor_copy(zl[:, :, P:T], cum2[:, :, P:T]).then_inc(dec_ready, 1)
                keep(n)
            n = len(LEVELS)
            dve.wait_ge(lv_ps, 2 * n + 2)
            dve.wait_ge(z_ready, n + 1)
            tt(kl[:, :, 0:P], k2[:, :, 0:P], zl[:, :, 0:P], ALU.mult)
            tt(ql[:, :, P:T], q2[:, :, P:T], zl[:, :, P:T], ALU.mult).then_inc(ql_ready, 1)
            keep(n)
            link(dve.memset(cm[:, :, 0:2], 0.0))
            dve.wait_ge(gc_ready, 2)
            for b in range(2):
                dve.wait_ge(hT_ps, 16 + b + 1)
                cols = slice(2 * b, 2 * b + 2)
                link(tt(cm[:, cols, 2:T + 2], gc[:, cols, :], bank[4 + b][:, :].rearrange("p (c n) -> p c n", c=2),
                        ALU.mult))
            dve.wait_ge(lv_ps, 2 * n + 3)
            dve.tensor_copy(att2.rearrange("p h n -> p (h n)"), bank[2][:, :]).then_inc(lv_ready, 1)
            dve.wait_ge(gb_ready, 2)
            for j in range(3):
                for c in range(CB):
                    w = vcol[:, 148 + j * CB + c:149 + j * CB + c]
                    if j == 0:
                        last = ts(gc[:, c, :], cm[:, c, 0:T], w, None, ALU.mult)
                    else:
                        last = stt(gc[:, c, :], cm[:, c, j:j + T], w, gc[:, c, :], ALU.mult, ALU.add)
                link(last)
            for c in range(CB):
                tt(gb[:, c, :], gb[:, c, :], gc[:, c, :], ALU.mult).then_inc(conv_ready, 1)
            dve.wait_ge(o2_sq, 1)
            dve.wait_ge(g_ready, 2)
            r = root(6, ss[:, 2:10], 1.0 / P, RMS_EPS)
            for t in range(NT):
                for h in range(HG):
                    cols = slice(h * P, (h + 1) * P)
                    last = stt(o_tok[:, t, cols], bank[t][:, cols], r[:, t * HG + h:t * HG + h + 1],
                               sg2[:, t, cols], ALU.mult, ALU.mult)
            last.then_inc(o2_ready, 1)

            def rms_residual(n, t, sums, banks, gain, base, dst, ready):
                link(tt(sq_sum[:, t:t + 1], sums[0], sums[1], ALU.add))
                r = root(n, sq_sum[:, t:t + 1], 1.0 / D, RMS_EPS)
                for g in range(2):
                    cols = slice(g * 512, (g + 1) * 512)
                    last = stt(dst[:, t, cols], bank[banks[g]][:, :], r, gain[:, cols],
                               ALU.mult, ALU.mult)
                link(last)
                tt(dst[:, t, :], dst[:, t, :], base[:, t, :], ALU.add).then_inc(ready, 1)

            dve.wait_ge(post_in, 32)
            for t in range(NT):
                dve.wait_ge(mix_sq, 2 * t + 2)
                rms_residual(7 + t, t, (ss2[:, 2 * t:2 * t + 1], ss2[:, 2 * t + 1:2 * t + 2]), (2 + 2 * t, 3 + 2 * t), row_g, x2, x3,
                             x3_ready)
            for t in range(NT):
                dve.wait_ge(x_sq, NT + t + 1)
                r = root(9 + t, ss2[:, 4 + t:5 + t], 1.0 / D, RMS_EPS)
                ts(xn[:, t, :], x3[:, t, :], r, None, ALU.mult).then_inc(xn_ready, 1)
            for b in (1, 3):
                dve.wait_ge(hT_ps, 18 + b + 1)
                for j in range(2):
                    c = 2 * b + j
                    ts(hT[:, c, :], bank[b][:, j * T:(j + 1) * T], vcol[:, 140 + c:141 + c], None, ALU.mult
                       ).then_inc(hT_dve, 1)
            for b in range(2):
                u = up_sb[:, b, :].rearrange("p (g n) -> p g n", g=2)
                link(dve.memset(u[:, :, 0:2], 0.0))
            for f in range(FB):
                dve.wait_ge(up_ready, f + 1)
                u = up_sb[:, f % 2, :].rearrange("p (g n) -> p g n", g=2)
                y = cv[:, f % 2, :].rearrange("p (g n) -> p g n", g=2)
                for j in range(3):
                    for g in range(2):
                        col = j * 2 * FB + g * FB + f
                        w = vcol[:, col:col + 1]
                        if j == 0:
                            last = ts(y[:, g, :], u[:, g, 0:T], w, None, ALU.mult)
                        else:
                            last = stt(y[:, g, :], u[:, g, j:j + T], w, y[:, g, :], ALU.mult, ALU.add)
                    if j < 2:
                        link(last)
                last.then_inc(cv_ready, 1)
                dve.wait_ge(cv_ready, f + 1)
                link(tt(y[:, 1, :], y[:, 1, :], y[:, 0, :], ALU.mult))
                dve.wait_ge(up_sig, f + 1)
                tt(aT[:, f, :], y[:, 1, :], sgt[:, f % 2, :], ALU.mult).then_inc(a_ready, 1)
            for t in range(NT):
                dve.wait_ge(down_sq, 2 * t + 2)
                rms_residual(11 + t, t, (ss2[:, 2 * t:2 * t + 1], ss2[:, 2 * t + 1:2 * t + 2]), (2 * t, 2 * t + 1), row_b, x3,
                             y_out, y_done)


_USED = ("x", "rel_bias", "a_w_in", "a_w_out", "ln_g", "ln_b", "moe_w_router", "moe_b_router", "moe_w_gate_up",
         "moe_b_gate_up", "moe_w_down", "moe_b_down", "w_in_2", "w_out_2", "conv_w_2", "ffn_w_up_2",
         "ffn_conv_w_2", "ffn_w_down_2", "hgrn_norm_g_2", "pre_mix_g_2", "post_mix_g_2", "pre_ffn_g_2",
         "post_ffn_g_2")
_WHOLE = ("rel_bias",)


def kernel(**inputs):
    import concourse.bacc as bacc
    from concourse.bass_utils import run_bass_kernel_spmd

    nc = bacc.Bacc("TRN2", target_bir_lowering=False, num_devices=1)
    arrays, args = {}, []
    for name in _USED:
        a = np.ascontiguousarray(inputs[name])
        arrays[f"in_{name}"] = a
        ap = nc.dram_tensor(f"in_{name}", a.shape, mybir.dt.from_np(a.dtype), kind="ExternalInput").ap()
        args.append(ap if name in _WHOLE else ap[0])
    for name, a in zip(("consts", "levels", "buckets", "behind"), shape_constants()):
        arrays[f"in_{name}"] = a
        args.append(nc.dram_tensor(f"in_{name}", a.shape, mybir.dt.float32, kind="ExternalInput").ap())
    args.append(nc.dram_tensor("rel_rows", (H, 2 * T), mybir.dt.float32, kind="Internal").ap())
    args.append(nc.dram_tensor("out", (1, T, D), mybir.dt.float32, kind="ExternalOutput").ap()[0])
    build(nc, *args)
    r = run_bass_kernel_spmd(nc, [arrays], core_ids=[0])
    return r.results[0]["out"]
```

```python
from contextlib import ExitStack

import numpy as np
import concourse.bass as bass
from concourse import mybir

P = 128
T, D = 256, 1024
NT = T // P
KC = D // P
H = 8
N_EXP, TOPK, FE = 32, 4, 1024
CAP = 64
ITEMS = N_EXP + (T * TOPK - N_EXP) // CAP + 1
ICOLS = ITEMS + 1
HG = 4
CB = 4
FF = 2816
FB = FF // P
UPG = FB // 2
LEVELS = (1, 2, 4, 8, 16, 32, 64)
ALPHA = 2.0 ** 0.25
LN_EPS, RMS_EPS = 1e-5, 1e-6
SWI_LIMIT, SWI_ALPHA = 7.0, 1.702
FAR = 16384.0
MASKED = -1e30
SLOT = 4096
SLOTS = 6
W2_SLOTS = 4
IN1, IN2, UP, DOWN, PIECES = 0, 12, 26, 26 + FB, 26 + FB + FB // 2

_C = {}
_c = 0
for _name, _width in (("ident", P), ("flip", P), ("before", P), ("ones", P), ("slot", P), ("expert", N_EXP),
                      ("item", ICOLS), ("item64", ICOLS), ("strict", P), ("incl", P), ("quarter", 4 * CAP),
                      ("thresholds", 4), ("first", 1), ("index", 1)):
    _C[_name] = (_c, _c + _width)
    _c += _width
CONSTS = _c


def shape_constants():
    c = np.zeros((P, CONSTS), np.float32)
    p = np.arange(P)

    def put(name, value):
        c[:, _C[name][0]:_C[name][1]] = value

    put("ident", np.eye(P))
    put("flip", np.eye(P)[::-1])
    put("before", p[:, None] < p[None, :])
    put("ones", 1.0)
    put("slot", p[None, :] % CAP)
    put("expert", np.arange(N_EXP)[None, :])
    put("item", np.arange(ICOLS)[None, :])
    put("item64", CAP * np.arange(ICOLS)[None, :])
    put("strict", (p[:, None] < p[None, :] % N_EXP) & (p[:, None] < N_EXP))
    put("incl", (p[:, None] <= p[None, :] % N_EXP) & (p[:, None] < N_EXP))
    put("quarter", p[:, None] // N_EXP == np.arange(4 * CAP)[None, :] // CAP)
    put("thresholds", CAP * np.arange(4)[None, :])
    put("first", (p == 0)[:, None])
    put("index", p[:, None])
    levels = np.zeros((P, 1 + len(LEVELS), P), np.float32)
    levels[:, 0] = np.eye(P)
    for n, m in enumerate(LEVELS):
        same = p[:, None] // (2 * m) == p[None, :] // (2 * m)
        levels[:, n + 1] = same & (p[:, None] % (2 * m) < m) & (p[None, :] % (2 * m) >= m)
    dist = T - 1 - np.arange(2 * T)
    far = np.maximum(dist, 1).astype(np.float32)
    large = 16 + (np.log(far / 16) / np.float32(np.log(8.0)) * 16).astype(np.int32)
    bucket = np.where(dist < 16, dist, np.minimum(large, 31))
    buckets = ((np.arange(32)[:, None] == bucket[None, :]) & (dist >= 0)[None, :]).astype(np.float32)
    behind = np.broadcast_to(np.where(dist < 0, MASKED, 0.0), (H, 2 * T)).astype(np.float32)
    return c, levels, buckets, np.ascontiguousarray(behind)


def build(nc, x, rel_bias, a_w_in, a_w_out, ln_g, ln_b, w_router, b_router, w_gu, b_gu, w_down, b_down,
          w_in2, w_out2, conv_w, ffn_up, ffn_conv, ffn_down, hgrn_g, pre_mix_g, post_mix_g, pre_ffn_g,
          post_ffn_g, consts, levels, buckets, behind, rel_rows, out):
    f32, i32, u32 = mybir.dt.float32, mybir.dt.int32, mybir.dt.uint32
    ALU, ACT, AX = mybir.AluOpType, mybir.ActivationFunctionType, mybir.AxisListType

    with ExitStack() as ctx:
        def sb(name, shape, dt=f32):
            return ctx.enter_context(nc.sbuf_tensor(name, shape, dt))

        def sem(name):
            return ctx.enter_context(nc.semaphore(name))

        ring = sb("ring", [P, SLOTS * SLOT])
        cst = sb("cst", [P, CONSTS])
        vrow_a = sb("vrow_a", [P, P])
        vrow_b = sb("vrow_b", [36, P])
        vcol = sb("vcol", [P, 164])
        arena = sb("arena", [P, 13720])
        f32r = mybir.dt.float32r
        w_hi, w_lo = sb("w_hi", [P, 2, 2048], f32r), sb("w_lo", [P, 2, 2048], f32r)
        x_hi, x_lo = sb("x_hi", [P, KC, T], f32r), sb("x_lo", [P, KC, T], f32r)
        bank = [ctx.enter_context(nc.psum_tensor(f"bank{b}", [P, 512], f32)) for b in range(8)]

        def const(name, rows=P):
            return cst[0:rows, _C[name][0]:_C[name][1]]

        def at(start, *dims, rows=P):
            size = int(np.prod(dims))
            v = arena[0:rows, start:start + size]
            if len(dims) == 2:
                v = v.rearrange("p (a b) -> p a b", a=dims[0])
            if len(dims) == 3:
                v = v.rearrange("p (a b c) -> p a b c", a=dims[0], b=dims[1])
            return v

        def slot(s, a):
            return ring[:, s * SLOT:(s + 1) * SLOT].rearrange("p (a b) -> p a b", a=a)

        ident, ones = const("ident"), const("ones")

        roots = [(n, 1) for n in range(6)] + [(6, 2 * HG)] + [(n + 7, 1) for n in range(7, 13)]
        variance, inv_root, newton = at(13612, 24), at(13636, 24), at(13660, 24)

        x_tok = at(0, NT, D)
        qT = at(2048, H, T)
        kT = at(4096, H, T)
        v_tok = at(6144, NT, D)
        bias = at(8192, H, 3 * P)
        prob = at(11264, 2, 3 * P)
        probT = at(12032, 2, 3 * P)
        oT = ring[:, 4 * SLOT:4 * SLOT + H * T].rearrange("p (h t) -> p h t", h=H)
        neg_max = at(12800, H, 2)
        prob_sum = at(12816, H, 2)
        prob_inv = at(12832, H, 2)
        rel_tab = at(11264, 512, rows=H)
        bucket_sb = at(11776, 512, rows=32)
        behind_sb = at(12288, 512, rows=H)
        relb_sb = at(12850, H, rows=32)
        stats = at(13690, NT, 2, 6)
        moments = at(13714, NT, 2)
        row_g = at(8192, D)
        row_b = at(9216, D)

        h1 = at(4096, NT, D)
        h1T = at(2048, KC, T)
        xeT = at(2048, KC, CAP)
        bias_sel = at(7168, 4, CAP)
        sel = at(7424, NT, CAP)
        selg = at(7552, NT, P)
        selgT = at(7808, NT, P)
        hg = at(0, 512)
        sig = at(512, 512)
        hu = at(1024, 512)
        act_e = at(1536, 4, P)
        actT = at(6144, 4, P)
        y_item = at(6656, 512)
        bgu = at(10240, 512)
        bdown = at(10752, D, rows=N_EXP)
        wr = at(11776, KC, N_EXP)
        br = at(12032, N_EXP)
        logit = at(12064, NT, N_EXP)
        top8 = at(12128, NT, 8)
        top_i = at(12144, NT, 8).bitcast(u32)
        top_f = at(12160, NT, 8)
        gate_e = at(12176, NT, TOPK)
        gate_s = at(12184, NT)
        gate_r = at(12186, NT)
        gate = at(12188, NT, TOPK)
        hit = at(12196, NT, TOPK, N_EXP)
        chosen = at(12452, NT, N_EXP)
        gates = at(12516, NT, N_EXP)
        place = at(12580, NT, N_EXP)
        count = at(12644, 1, rows=N_EXP)
        over = at(12645, 4, rows=N_EXP)
        blocks = at(12649, 1, rows=N_EXP)
        span = at(12650, 2)
        span64 = at(12652, 1, rows=N_EXP)
        from_first = at(12653, ICOLS)
        owner = at(12712, ICOLS)
        gatesT = at(12816, T, rows=N_EXP)
        placeT = at(13072, T, rows=N_EXP)
        item_place = at(13328, NT, ICOLS)
        item_gate = at(13440, NT, ICOLS)
        item_exp = at(13552, ICOLS + 1, rows=1).bitcast(i32)

        x2 = at(0, NT, D)
        xn = at(2048, NT, D)
        gc = at(2048, CB, T)
        cm = at(3072, CB, T + 2)
        q2 = at(4112, HG, T)
        lf = at(5136, HG, T)
        k2 = at(6160, HG, T)
        cum = at(7184, HG, T)
        cum2 = at(8208, HG, T)
        v2 = at(9232, NT, 512)
        sg2 = at(10256, NT, 512)
        ss = at(11284, 16)
        ss2 = at(11300, 16)
        sq_sum = at(11316, 16)
        post_g = at(11340, D)
        post_b = at(12364, D)

        def scratch(start, *dims):
            start += W2_SLOTS * SLOT
            v = ring[:, start:start + int(np.prod(dims))]
            return v.rearrange("p (a b) -> p a b", a=dims[0]) if len(dims) == 2 else v

        zl = scratch(0, HG, T)
        kl = scratch(1024, HG, T)
        ql = scratch(2048, HG, T)
        o_tok = scratch(0, NT, 512)
        att = scratch(3072, 8, P)
        att2 = scratch(4096, HG, P)
        lev = scratch(4608, 1 + len(LEVELS), P)
        gb = scratch(5632, CB, T)
        mixT = scratch(6656, HG, T)
        x3 = at(4112, NT, D)
        aT = scratch(0, FB, T)
        up_sb = scratch(5632, 2, 2 * (T + 2))
        cv = scratch(6664, 2, 2 * T)
        sgt = at(10400, 2, T)
        y_out = at(2048, NT, D)

        x_in, const_in, rel_in, vrow_in = sem("x_in"), sem("const_in"), sem("rel_in"), sem("vrow_in")
        attn_w = [sem(f"attn_w{s}") for s in range(8)]
        hi_ready, lo_ready, piece_used = sem("hi_ready"), sem("lo_ready"), sem("piece_used")
        a_hi_ready, a_lo_ready = sem("a_hi_ready"), sem("a_lo_ready")
        moe_w = [sem(f"moe_w{s}") for s in range(6)]
        w2_in = [sem(f"w2_in{s}") for s in range(W2_SLOTS)]
        ln0_in, ln1_in, post_in = sem("ln0_in"), sem("ln1_in"), sem("post_in")
        rel_stored, bias_in = sem("rel_stored"), sem("bias_in")
        moe_small_in, lev_in = sem("moe_small_in"), sem("lev_in")
        rel_ps, rel_ready = sem("rel_ps"), sem("rel_ready")
        vcol_ps, vcol_ready = sem("vcol_ps"), sem("vcol_ready")
        xT_ps, xT_hi, xT_lo = sem("xT_ps"), sem("xT_hi"), sem("xT_lo")
        proj_ps, proj_act, proj_dve = sem("proj_ps"), sem("proj_act"), sem("proj_dve")
        s_ps, max_ready, exp_ready = sem("s_ps"), sem("max_ready"), sem("exp_ready")
        prob_ready, pt_ps, pt_ready, o_ps, o_ready = (sem("prob_ready"), sem("pt_ps"), sem("pt_ready"),
                                                      sem("o_ps"), sem("o_ready"))
        out_ps, h1_ready = sem("out_ps"), sem("h1_ready")
        h1T_ps, h1T_act, h1T_dve = sem("h1T_ps"), sem("h1T_act"), sem("h1T_dve")
        logit_ps, top_ready, gexp_ready = sem("logit_ps"), sem("top_ready"), sem("gexp_ready")
        route_ready, pos_ps, blocks_ready = sem("route_ready"), sem("pos_ps"), sem("blocks_ready")
        span_ps, owner_ready, items_ps, items_ready = (sem("span_ps"), sem("owner_ready"), sem("items_ps"),
                                                       sem("items_ready"))
        w_used = [sem(f"w_used{s}") for s in range(6)]
        gath_ps, xe_ready = sem("gath_ps"), sem("xe_ready")
        sel_ready, selg_ready, bsel_ready = sem("sel_ready"), sem("selg_ready"), sem("bsel_ready")
        hg_ready, gu_read, sig_ready, act_ready = (sem("hg_ready"), sem("gu_read"), sem("sig_ready"),
                                                   sem("act_ready"))
        actT_ps, actT_ready, selgT_ps, selgT_ready = (sem("actT_ps"), sem("actT_ready"), sem("selgT_ps"),
                                                      sem("selgT_ready"))
        y_ready, prod_ready, moe_done = sem("y_ready"), sem("prod_ready"), sem("moe_done")
        var_ready, rough_ready = sem("var_ready"), sem("rough_ready")
        x2_ready, xn_ready = sem("x2_ready"), sem("xn_ready")
        hT_ps, hT_hi, hT_lo = sem("hT_ps"), sem("hT_hi"), sem("hT_lo")
        r2_ps = sem("r2_ps")
        f_abs, lf_ready, lfm_ready, k_ready = sem("f_abs"), sem("lf_ready"), sem("lfm_ready"), sem("k_ready")
        f_log = sem("f_log")
        q_sig, q_ready, g_sig, g_ready, v_ready = (sem("q_sig"), sem("q_ready"), sem("g_sig"), sem("g_ready"),
                                                   sem("v_ready"))
        gb_ready, gc_ready, ch_read, conv_ready = sem("gb_ready"), sem("gc_ready"), sem("ch_read"), sem("conv_ready")
        dec_ready, z_ready, ql_ready = sem("dec_ready"), sem("z_ready"), sem("ql_ready")
        lv_ps, lv_ready, o2_ps, o2_sq, o2_ready = (sem("lv_ps"), sem("lv_ready"), sem("o2_ps"), sem("o2_sq"),
                                                   sem("o2_ready"))
        mT_ps, mT_ready, mix_ps, mix_sq, x3_ready = (sem("mT_ps"), sem("mT_ready"), sem("mix_ps"), sem("mix_sq"),
                                                     sem("x3_ready"))
        x_sq, up_ps, up_ready, up_sig, a_ready = (sem("x_sq"), sem("up_ps"), sem("up_ready"), sem("up_sig"),
                                                  sem("a_ready"))
        cv_ready, cv_tap, a_prod = sem("cv_ready"), sem("cv_tap"), sem("a_prod")
        down_ps, down_sq, y_done, out_done = sem("down_ps"), sem("down_sq"), sem("y_done"), sem("out_done")
        dve_step, act_step = sem("dve_step"), sem("act_step")

        class Link:

            def __init__(self, eng, step):
                self.eng, self.step, self.n = eng, step, 0

            def __call__(self, ins):
                self.n += 1
                ins.then_inc(self.step, 1)
                self.eng.wait_ge(self.step, self.n)

        def row(v, n):
            return v.rearrange("(a n) -> a n", a=1).to_broadcast([P, n])

        w2_loads = []

        def w2_slot():
            return len(w2_loads) % W2_SLOTS

        for g in (1, 0, 2, 3, 4, 5, 6):
            s = w2_slot()
            w2_loads.append((s, [(slot(s, KC), w_in2[:, g * 512:(g + 1) * 512].rearrange("(c p) n -> p c n", p=P))]))
        for g in range(2):
            s = w2_slot()
            w2_loads.append((s, [(slot(s, KC), w_out2[:, g * 512:(g + 1) * 512].rearrange("(c p) n -> p c n", p=P))]))
        for g in range(UPG):
            s = w2_slot()
            w2_loads.append((s, [(slot(s, KC)[:, :, j * 256:(j + 1) * 256],
                                  ffn_up[:, j * FF + g * 256:j * FF + (g + 1) * 256].rearrange("(c p) n -> p c n", p=P))
                                 for j in range(2)]))
        for g in range(-(-FB // 4)):
            s = w2_slot()
            k = min(4, FB - 4 * g)
            w2_loads.append((s, [(slot(s, 4)[:, 0:k, :],
                                  ffn_down[g * 512:g * 512 + k * P, :].rearrange("(c p) n -> p c n", p=P))]))

        w2_count, seen = [], [0] * W2_SLOTS
        for s, parts in w2_loads:
            seen[s] += 16 * len(parts)
            w2_count.append(seen[s])

        pieces = [(attn_w[p // 2], 16, slot(p // 2, KC)[:, :, (p % 2) * 256:(p % 2 + 1) * 256]) for p in range(12)]
        for n in range(7):
            s = w2_loads[n][0]
            pieces += [(w2_in[s], w2_count[n], slot(s, KC)[:, :, j * 256:(j + 1) * 256]) for j in range(2)]
        for n in range(9, 9 + UPG):
            s = w2_loads[n][0]
            pieces += [(w2_in[s], w2_count[n],
                        slot(s, KC).rearrange("p c (g n) -> p c g n", g=2)[:, :, :, j * P:(j + 1) * P])
                       for j in range(2)]
        for p in range(FB // 2):
            n = 9 + UPG + p // 2
            s = w2_loads[n][0]
            pieces.append((w2_in[s], w2_count[n], slot(s, 4)[:, 2 * (p % 2):2 * (p % 2) + 2, :]))
        assert len(pieces) == PIECES

        def like(buffer, p):
            v = buffer[:, p % 2, :]
            if p >= DOWN:
                return v.rearrange("p (c n) -> p c n", c=2)
            if p >= UP:
                return v.rearrange("p (c g n) -> p c g n", c=KC, g=2)
            return v.rearrange("p (c n) -> p c n", c=KC)

        block = ctx.enter_context(nc.Block())

        @block.sync
        def _(sp):
            sp.dma_start(x_tok, x.rearrange("(t p) d -> p t d", p=P)).then_inc(x_in, 16)
            sp.dma_start(cst[:, :], consts[:, :]).then_inc(const_in, 16)
            for s in range(6):
                sp.dma_start(slot(s, KC), a_w_in[:, s * 512:(s + 1) * 512].rearrange("(c p) n -> p c n", p=P)
                             ).then_inc(attn_w[s], 16)
            for g in range(2):
                sp.wait_ge(lo_ready, 2 * g + 2)
                sp.dma_start(slot(g, KC), a_w_out[:, g * 512:(g + 1) * 512].rearrange("(c p) n -> p c n", p=P)
                             ).then_inc(attn_w[6 + g], 16)

            def load_expert(e, wait_slot, order=range(6)):
                for s in order:
                    wait_slot(s)
                    if s < 4:
                        src = w_gu[bass.ds(e, 1), s * 256:(s + 1) * 256, :].rearrange("o (c p) n -> p (o c) n", p=P)
                        dst = slot(s, 2)
                    else:
                        src = w_down[bass.ds(e, 1), (s - 4) * 512:(s - 3) * 512, :].rearrange(
                            "o (c p) n -> p (o c) n", p=P)
                        dst = slot(s, 4)
                    sp.dma_start(dst, src).then_inc(moe_w[s], 16)

            load_expert(0, lambda s: sp.wait_ge(*((out_ps, 4) if s in (0, 1, 4) else (lo_ready, 2 * s + 2))),
                        (2, 3, 5, 0, 1, 4))
            sp.wait_ge(items_ready, 1)
            n_items = sp.value_load(item_exp[0:1, ICOLS:ICOLS + 1], min_val=1, max_val=ITEMS)
            with sp.Fori(1, ITEMS) as i:
                with sp.If(i < n_items):
                    e = sp.value_load(item_exp[0:1, bass.ds(i, 1)], min_val=0, max_val=N_EXP - 1)
                    load_expert(e, lambda s: sp.wait_ge(w_used[s], i))
            def wait_used(n):
                if n < 7:
                    sp.wait_ge(lo_ready, IN2 + 2 * (n + 1))
                elif n < 9:
                    sp.wait_ge(mix_ps, n - 4)
                else:
                    sp.wait_ge(lo_ready, UP + 2 * (n - 9 + 1))

            sp.wait_ge(moe_done, 1)
            for n, (s, parts) in enumerate(w2_loads):
                if n >= W2_SLOTS:
                    wait_used(n - W2_SLOTS)
                for dst, src in parts:
                    sp.dma_start(dst, src).then_inc(w2_in[s], 16)
            for t in range(NT):
                sp.wait_ge(y_done, t + 1)
                sp.dma_start(out[t * P:(t + 1) * P, :], y_out[:, t, :]).then_inc(out_done, 16)
            sp.wait_ge(out_done, 16 * NT)

        @block.gpsimd
        def _(pool):
            pool.dma_start(bucket_sb, buckets[:, :]).then_inc(rel_in, 16)
            pool.dma_start(behind_sb, behind[:, :]).then_inc(rel_in, 16)
            pool.dma_start(relb_sb, rel_bias[:, :]).then_inc(rel_in, 16)
            fc = ffn_conv.rearrange("j (f p) -> (j f) p", p=P)
            pool.dma_start(vrow_a[:, :], fc[0:P, :]).then_inc(vrow_in, 16)
            pool.dma_start(vrow_b[0:4, :], fc[P:132, :]).then_inc(vrow_in, 16)
            for start, rows, src in ((4, 8, pre_mix_g), (12, 8, pre_ffn_g)):
                pool.dma_start(vrow_b[start:start + rows, :], src.rearrange("(c p) -> c p", p=P)).then_inc(vrow_in, 16)
            pool.dma_start(vrow_b[20:32, :], conv_w.rearrange("j (c p) -> (j c) p", p=P)).then_inc(vrow_in, 16)
            pool.dma_start(vrow_b[32:36, :], hgrn_g.rearrange("(c p) -> c p", p=P)).then_inc(vrow_in, 16)
            pool.wait_ge(rel_ready, 1)
            pool.dma_start(rel_rows[:, :], rel_tab).then_inc(rel_stored, 16)
            pool.wait_ge(rel_stored, 16)
            rel_t = rel_rows.tensor
            pool.dma_start(bias[:, :, 0:P], bass.AP(rel_t, P, [[1, P], [2 * T, H], [1, P]])).then_inc(bias_in, 16)
            pool.dma_start(bias[:, :, P:3 * P], bass.AP(rel_t, 0, [[1, P], [2 * T, H], [1, 2 * P]])
                           ).then_inc(bias_in, 16)
            pool.wait_ge(prob_ready, H)
            pool.wait_ge(pt_ps, H)
            pool.dma_start(row_g, row(ln_g[0, :], D)).then_inc(ln0_in, 16)
            pool.dma_start(row_b, row(ln_b[0, :], D)).then_inc(ln0_in, 16)
            pool.wait_ge(o_ps, H)
            pool.dma_start(wr, w_router.rearrange("(c p) e -> p c e", p=P)).then_inc(moe_small_in, 16)
            pool.dma_start(br, row(b_router, N_EXP)).then_inc(moe_small_in, 16)
            for q in range(4):
                pool.dma_start(bgu[q * 32:(q + 1) * 32, :], b_gu[:, q * 512:(q + 1) * 512]).then_inc(moe_small_in, 16)
            pool.dma_start(bdown, b_down[:, :]).then_inc(moe_small_in, 16)
            pool.wait_ge(h1_ready, NT)
            pool.dma_start(row_g, row(ln_g[1, :], D)).then_inc(ln1_in, 16)
            pool.dma_start(row_b, row(ln_b[1, :], D)).then_inc(ln1_in, 16)
            pool.wait_ge(moe_done, 1)
            pool.dma_start(lev, levels[:, :, :]).then_inc(lev_in, 16)
            pool.wait_ge(x2_ready, NT)
            pool.dma_start(post_g, row(post_mix_g, D)).then_inc(post_in, 16)
            pool.dma_start(post_b, row(post_ffn_g, D)).then_inc(post_in, 16)
            for f in range(FB):
                pool.wait_ge(cv_ready, f + 1)
                y = cv[:, f % 2, :].rearrange("p (g n) -> p g n", g=2)
                pool.tensor_tensor(aT[:, f, :], y[:, 1, :], y[:, 0, :], ALU.mult).then_inc(a_prod, 1)
                pool.wait_ge(a_prod, f + 1)
                pool.wait_ge(up_sig, f + 1)
                pool.tensor_tensor(aT[:, f, :], aT[:, f, :], sgt[:, f % 2, :], ALU.mult).then_inc(a_ready, 1)

        @block.tensor
        def _(pe):
            mm = pe.matmul

            def turn(dst, src, rows=P):
                return pe.transpose(dst, src, ident[0:rows, 0:rows])

            pe.wait_ge(const_in, 16)
            pe.wait_ge(x_in, 16)
            for t in range(NT):
                for g in range(2):
                    b = 2 * t + g
                    for j in range(4):
                        last = turn(bank[b][:, j * P:(j + 1) * P], x_tok[:, t, (4 * g + j) * P:(4 * g + j + 1) * P])
                    last.then_inc(xT_ps, 1)
            def product(p, dst, tokens_stationary=False):
                pe.wait_ge(lo_ready, p + 1)
                hi, lo = (v[:, p % 2, :].rearrange("p (c n) -> p c n", c=KC) for v in (w_hi, w_lo))
                for j in range(2):
                    part = slice(j * P, (j + 1) * P)
                    for c in range(KC):
                        for n, (w, a) in enumerate(((hi, x_hi), (hi, x_lo), (lo, x_hi))):
                            lhs, rhs = (a[:, c, part], w[:, c, :]) if tokens_stationary else (w[:, c, part], a[:, c, :])
                            last = mm(dst[:, j * T:(j + 1) * T], lhs, rhs, start=c == 0 and n == 0,
                                      stop=c == KC - 1 and n == 2)
                    yield last

            pe.wait_ge(xT_hi, 4)
            pe.wait_ge(xT_lo, 4)
            for r in range(12):
                b = (4 + r) % 8
                if r == 9:
                    pe.wait_ge(rel_in, 48)
                    pe.wait_ge(proj_act, 3)
                    mm(bank[0][0:H, :], relb_sb, bucket_sb, start=True, stop=True).then_inc(rel_ps, 1)
                    pe.wait_ge(vrow_in, 96)
                    pe.wait_ge(proj_dve, 3)
                    turn(bank[1][:, 0:P], vrow_a[:, :])
                    turn(bank[1][:, P:P + 36], vrow_b[:, :], 36).then_inc(vcol_ps, 1)
                if r >= 8:
                    pe.wait_ge(proj_dve if r % 2 else proj_act, (r - 8) // 2 + 1)
                for last in product(IN1 + r, bank[b], r >= 8):
                    pass
                last.then_inc(proj_ps, 1)

            def scores(h):
                if h >= 2:
                    pe.wait_ge(exp_ready, h - 1)
                b = bank[h % 2]
                mm(b[:, 0:3 * P], const("flip"), bias[:, h, :], start=True, stop=True)
                mm(b[:, 0:P], qT[:, h, 0:P], kT[:, h, 0:P], start=False, stop=True, skip_group_check=True)
                mm(b[:, P:3 * P], qT[:, h, P:T], kT[:, h, :], start=False, stop=True,
                   skip_group_check=True).then_inc(s_ps, 1)

            def turn_probs(h):
                pe.wait_ge(prob_ready, h + 1)
                if h >= 2:
                    pe.wait_ge(pt_ready, h - 1)
                b, p = bank[2 + h % 2], prob[:, h % 2, :]
                for j in range(3):
                    last = turn(b[:, j * P:(j + 1) * P], p[:, j * P:(j + 1) * P])
                last.then_inc(pt_ps, 1)

            def values(h):
                pe.wait_ge(pt_ready, h + 1)
                if h >= 2:
                    pe.wait_ge(o_ready, h - 1)
                b, p = bank[4 + h % 2], probT[:, h % 2, :]
                mm(b[:, 0:T], v_tok[:, 0, h * P:(h + 1) * P], p[:, 0:T], start=True, stop=True)
                mm(b[:, P:T], v_tok[:, 1, h * P:(h + 1) * P], p[:, T:3 * P], start=False, stop=True,
                   skip_group_check=True).then_inc(o_ps, 1)

            pe.wait_ge(proj_act, 6)
            pe.wait_ge(proj_dve, 6)
            pe.wait_ge(bias_in, 32)
            pe.wait_ge(vcol_ready, 1)
            scores(0)
            scores(1)
            for h in range(H):
                turn_probs(h)
                if h + 2 < H:
                    scores(h + 2)
                values(h)
            pe.wait_ge(o_ready, H)
            for t in range(NT):
                for g in range(2):
                    pe.wait_ge(attn_w[6 + g], 16)
                    for h in range(H):
                        last = mm(bank[2 * g + t][:, :], oT[:, h, t * P:(t + 1) * P], slot(g, KC)[:, h, :],
                                  start=h == 0, stop=h == H - 1)
                    last.then_inc(out_ps, 1)

            for t in range(NT):
                pe.wait_ge(h1_ready, t + 1)
                for g in range(2):
                    b = 4 + 2 * t + g
                    for j in range(4):
                        last = turn(bank[b][:, j * P:(j + 1) * P], h1[:, t, (4 * g + j) * P:(4 * g + j + 1) * P])
                    last.then_inc(h1T_ps, 1)
            pe.wait_ge(h1T_act, 2)
            pe.wait_ge(h1T_dve, 2)
            pe.wait_ge(moe_small_in, 7 * 16)
            for t in range(NT):
                for c in range(KC):
                    last = mm(bank[0][:, t * N_EXP:(t + 1) * N_EXP], h1T[:, c, t * P:(t + 1) * P], wr[:, c, :],
                              start=c == 0, stop=c == KC - 1)
            last.then_inc(logit_ps, 1)
            pe.wait_ge(route_ready, 1)
            before = const("before")
            mm(bank[1][:, 0:N_EXP], before, chosen[:, 0, :], start=True, stop=True)
            mm(bank[1][:, N_EXP:2 * N_EXP], ones, chosen[:, 0, :], start=True, stop=False)
            mm(bank[1][:, N_EXP:2 * N_EXP], before, chosen[:, 1, :], start=False, stop=True)
            for t in range(NT):
                mm(bank[2][0:N_EXP, 0:1], chosen[:, t, :], ones[:, 0:1], start=t == 0, stop=t == NT - 1)
            for t in range(NT):
                last = turn(bank[3][0:N_EXP, t * P:(t + 1) * P], gates[:, t, :])
            last.then_inc(pos_ps, 1)
            pe.wait_ge(blocks_ready, 1)
            mm(bank[0][:, 0:1], const("strict", N_EXP), blocks, start=True, stop=True)
            mm(bank[0][:, 1:2], const("incl", N_EXP), blocks, start=True, stop=True)
            for t in range(NT):
                last = turn(bank[1][0:N_EXP, t * P:(t + 1) * P], place[:, t, :])
            last.then_inc(span_ps, 1)
            pe.wait_ge(owner_ready, 1)
            own = owner[0:N_EXP, :]
            for t in range(NT):
                mm(bank[2][:, t * ICOLS:(t + 1) * ICOLS], placeT[:, t * P:(t + 1) * P], own, start=True, stop=True)
            for t in range(NT):
                mm(bank[3][:, t * ICOLS:(t + 1) * ICOLS], gatesT[:, t * P:(t + 1) * P], own, start=True, stop=True)
            mm(bank[0][0:1, 0:ICOLS], const("index", N_EXP), own, start=True, stop=True)
            mm(bank[0][0:1, ICOLS:ICOLS + 1], ones[0:N_EXP, 0:1], blocks, start=True, stop=True)
            for g in range(2):
                for t in range(NT):
                    last = mm(bank[4 + 2 * g + t][:, :], gatesT[:, t * P:(t + 1) * P], bdown[:, g * 512:(g + 1) * 512],
                              start=True, stop=True)
            last.then_inc(items_ps, 1)

            def gather():
                for c in range(KC):
                    for t in range(NT):
                        last = mm(bank[2][:, c * CAP:(c + 1) * CAP], h1[:, t, c * P:(c + 1) * P], sel[:, t, :],
                                  start=t == 0, stop=t == NT - 1)
                last.then_inc(gath_ps, 1)

            pe.wait_ge(sel_ready, 1)
            pe.wait_ge(items_ready, 1)
            gather()
            n_items = pe.value_load(item_exp[0:1, ICOLS:ICOLS + 1], min_val=1, max_val=ITEMS)
            with pe.Fori(0, ITEMS) as i:
                with pe.If(i < n_items):
                    pe.wait_ge(xe_ready, i + 1)
                    pe.wait_ge(bsel_ready, i + 1)
                    pe.wait_ge(gu_read, i + 1)
                    pe.wait_ge(y_ready, i + 1)
                    for q in range(4):
                        half = q % 2
                        mm(bank[q // 2][half * 64:half * 64 + 64, :], bias_sel[:, q, :], bgu, start=True, stop=False)
                    for c in range(KC):
                        if c % 2 == 0:
                            pe.wait_ge(moe_w[c // 2], i * 16 + 16)
                        w = slot(c // 2, 2)
                        for q in range(4):
                            half = q % 2
                            last = mm(bank[q // 2][half * 64:half * 64 + 64, :], xeT[:, c, :],
                                      w[:, c % 2, q * 512:(q + 1) * 512], start=False, stop=c == KC - 1)
                        if c % 2 == 1:
                            last.then_inc(w_used[c // 2], 1)
                    pe.wait_ge(sel_ready, i + 2)
                    pe.wait_ge(selgT_ready, i + 1)
                    gather()
                    pe.wait_ge(act_ready, i + 1)
                    for c in range(4):
                        last = turn(bank[3][:, c * P:(c + 1) * P], act_e[:, c, :])
                    last.then_inc(actT_ps, 1)
                    pe.wait_ge(selg_ready, i + 1)
                    pe.wait_ge(xe_ready, i + 2)
                    for t in range(NT):
                        last = turn(bank[2][:, t * P:(t + 1) * P], selg[:, t, :])
                    last.then_inc(selgT_ps, 1)
                    pe.wait_ge(actT_ready, i + 1)
                    for c in range(KC):
                        if c % 4 == 0:
                            pe.wait_ge(moe_w[4 + c // 4], i * 16 + 16)
                        lhs = actT[:, c % 4, (c // 4) * 64:(c // 4) * 64 + 64]
                        w = slot(4 + c // 4, 4)
                        for half in range(2):
                            last = mm(bank[1][half * 64:half * 64 + 64, :], lhs,
                                      w[:, c % 4, half * 512:(half + 1) * 512], start=c == 0, stop=c == KC - 1)
                        if c % 4 == 3:
                            last.then_inc(w_used[4 + c // 4], 1)
                    pe.wait_ge(y_ready, i + 2)
                    pe.wait_ge(selgT_ready, i + 2)
                    for t in range(NT):
                        for half in range(2):
                            rows = slice(half * 64, half * 64 + 64)
                            mm(bank[4 + 2 * half + t][:, :], selgT[rows, t, :], y_item[rows, :],
                               start=False, stop=True, skip_group_check=True)
            pe.drain().then_inc(moe_done, 1)

            def turn_tokens(src, ready, ps):
                for t in range(NT):
                    pe.wait_ge(*ready(t))
                for b in range(4):
                    for j in range(2):
                        for t in range(NT):
                            last = turn(bank[b][:, j * T + t * P:j * T + (t + 1) * P],
                                        src[:, t, (2 * b + j) * P:(2 * b + j + 1) * P])
                    last.then_inc(ps, 1)

            def w2_wait(n):
                pe.wait_ge(w2_in[w2_loads[n][0]], w2_count[n])
                return slot(w2_loads[n][0], KC)

            turn_tokens(xn, lambda t: (xn_ready, t + 1), hT_ps)
            pe.wait_ge(hT_hi, KC)
            pe.wait_ge(hT_lo, KC)
            for r in range(8):
                for last in product(IN2 + r, bank[r], r >= 4):
                    pass
                last.then_inc(r2_ps, 1)

            def level(n):
                if n == 0:
                    pe.wait_ge(k_ready, 2)
                    pe.wait_ge(q_ready, 2)
                    pe.wait_ge(g_ready, 2)
                else:
                    pe.wait_ge(ql_ready, n)
                    pe.wait_ge(lv_ready, n)
                ks, qs = (k2, q2) if n == 0 else (kl, ql)
                for b in range(2):
                    for j in range(4):
                        h, t = 2 * b + j // 2, j % 2
                        last = mm(bank[6 + b][:, j * P:(j + 1) * P], ks[:, h, t * P:(t + 1) * P],
                                  qs[:, h, t * P:(t + 1) * P], start=True, stop=True)
                    last.then_inc(lv_ps, 1)

            done = 0
            for r in range(8, 14):
                pe.wait_ge(*((lfm_ready, 2), (q_ready, 2), (v_ready, 2))[(r - 8) // 2])
                for j, last in enumerate(product(IN2 + r, bank[r - 8])):
                    if j == 1:
                        last.then_inc(r2_ps, 1)
                    if 2 * (r - 8) + j >= 3 and done <= len(LEVELS):
                        level(done)
                        done += 1
            assert done == 1 + len(LEVELS)
            pe.wait_ge(ql_ready, len(LEVELS) + 1)
            pe.wait_ge(gc_ready, 2)
            for h in range(HG):
                last = mm(bank[2][:, h * P:(h + 1) * P], kl[:, h, 0:P], ql[:, h, P:T], start=True, stop=True)
            last.then_inc(lv_ps, 1)
            pe.wait_ge(lv_ready, len(LEVELS) + 2)
            pe.wait_ge(gb_ready, 2)
            pe.wait_ge(v_ready, 2)
            for h in range(HG):
                mm(bank[0][:, h * P:(h + 1) * P], att[:, 2 * h, :], v2[:, 0, h * P:(h + 1) * P], start=True, stop=True)
                mm(bank[1][:, h * P:(h + 1) * P], att[:, 2 * h + 1, :], v2[:, 1, h * P:(h + 1) * P],
                   start=True, stop=False)
                last = mm(bank[1][:, h * P:(h + 1) * P], att2[:, h, :], v2[:, 0, h * P:(h + 1) * P],
                          start=False, stop=True)
            last.then_inc(o2_ps, 1)
            def mix(t, g, chunks):
                w = slot(w2_loads[7 + g][0], KC)
                for c in chunks:
                    lhs = mixT[:, c, t * P:(t + 1) * P] if c < HG else gb[:, c - HG, t * P:(t + 1) * P]
                    last = mm(bank[2 + 2 * t + g][:, :], lhs, w[:, c, :], start=c == HG, stop=c == HG - 1)
                return last

            pe.wait_ge(conv_ready, CB)
            for g in range(2):
                w2_wait(7 + g)
                for t in range(NT):
                    mix(t, g, range(HG, KC))
            pe.wait_ge(o2_ready, 1)
            for g in range(2):
                for j in range(2):
                    for t in range(NT):
                        h = 2 * g + j
                        last = turn(bank[6 + g][:, j * T + t * P:j * T + (t + 1) * P],
                                    o_tok[:, t, h * P:(h + 1) * P])
                last.then_inc(mT_ps, 1)
            pe.wait_ge(mT_ready, 4)
            for t in range(NT):
                for g in range(2):
                    mix(t, g, range(HG)).then_inc(mix_ps, 1)
            pe.wait_ge(x3_ready, NT)
            turn_tokens(xn, lambda t: (xn_ready, NT + t + 1), hT_ps)
            pe.wait_ge(hT_hi, 2 * KC)
            pe.wait_ge(hT_lo, 2 * KC)
            for f in range(FB):
                if f >= 2:
                    pe.wait_ge(up_ready, f - 1)
                for last in product(UP + f, bank[4 + f % 2]):
                    pass
                last.then_inc(up_ps, 1)

            def down(c, t):
                n = (DOWN + c // 2) % 2
                hi, lo = (v[:, n, (c % 2) * D:(c % 2 + 1) * D] for v in (w_hi, w_lo))
                part = slice(t * P, (t + 1) * P)
                a_hi, a_lo = x_hi[:, c % KC, part], x_lo[:, c % KC, part]
                for g in range(2):
                    cols = slice(g * 512, (g + 1) * 512)
                    for k, (a, w) in enumerate(((a_hi, hi), (a_hi, lo), (a_lo, hi))):
                        last = mm(bank[2 * t + g][:, :], a, w[:, cols], start=c == 0 and k == 0,
                                  stop=c == FB - 1 and k == 2)
                return last

            for p in range(FB // 2):
                pe.wait_ge(lo_ready, DOWN + p + 1)
                pe.wait_ge(a_lo_ready, p + 1)
                if p < FB // 2 - 1:
                    for c in (2 * p, 2 * p + 1):
                        for t in range(NT):
                            last = down(c, t)
                    last.then_inc(piece_used, 1)
                else:
                    for t in range(NT):
                        down(2 * p, t)
                        down(2 * p + 1, t).then_inc(down_ps, 1)

        @block.scalar
        def _(act):
            link = Link(act, act_step)
            copy = nc.scalar.copy
            activate = nc.scalar.activation

            def rough_root(n):
                c, k = roots[n]
                act.wait_ge(var_ready, n + 1)
                link(activate(inv_root[:, c:c + k], variance[:, c:c + k], ACT.Ln))
                activate(inv_root[:, c:c + k], inv_root[:, c:c + k], ACT.Exp, scale=-0.5).then_inc(rough_ready, 1)

            def split_hi(p):
                act.wait_ge(pieces[p][0], pieces[p][1])
                if IN1 + 2 <= p < IN2:
                    act.wait_ge(proj_ps, p - IN1 - 1)
                elif IN2 + 2 <= p < UP:
                    act.wait_ge(r2_ps, p - IN2 - 1)
                elif UP + 2 <= p < DOWN + 2:
                    act.wait_ge(up_ps, p - UP - 1)
                elif p >= DOWN + 2:
                    act.wait_ge(piece_used, p - DOWN - 1)
                copy(like(w_hi, p), pieces[p][2]).then_inc(hi_ready, 1)

            def evict_hi(first, gain):
                for c in range(KC):
                    if c % 2 == 0:
                        act.wait_ge(hT_ps, first + c // 2 + 1)
                    activate(x_hi[:, c, :], bank[c // 2][:, c % 2 * T:(c % 2 + 1) * T], ACT.Copy,
                             scale=vcol[:, gain + c:gain + c + 1]).then_inc(hT_hi, 1)

            for t in range(NT):
                for g in range(2):
                    b = 2 * t + g
                    act.wait_ge(xT_ps, b + 1)
                    copy(x_hi[:, 4 * g:4 * g + 4, t * P:(t + 1) * P],
                         bank[b][:, :].rearrange("p (c n) -> p c n", c=4)).then_inc(xT_hi, 1)
            split_hi(IN1)
            split_hi(IN1 + 1)
            for r in range(12):
                if r + 2 < 12:
                    split_hi(IN1 + r + 2)
                if r % 2:
                    continue
                act.wait_ge(proj_ps, r + 1)
                src = bank[(4 + r) % 8][:, :].rearrange("p (c n) -> p c n", c=2)
                if r < 8:
                    dst, h = (qT, r) if r < 4 else (kT, r - 4)
                    scale = float(P) ** -0.5 if r < 4 else 1.0
                    activate(dst[:, 2 * h:2 * h + 2, :], src, ACT.Copy, scale=scale).then_inc(proj_act, 1)
                else:
                    copy(v_tok[:, :, (r - 8) * 256:(r - 7) * 256], src).then_inc(proj_act, 1)
            for h in range(H + 1):
                if h < H:
                    act.wait_ge(max_ready, h + 1)
                    if h >= 2:
                        act.wait_ge(pt_ps, h - 1)
                    p, s = prob[:, h % 2, :], bank[h % 2]
                    activate(p[:, 0:P], s[:, 0:P], ACT.Exp, bias=neg_max[:, h, 0:1], accum_out=prob_sum[:, h, 0:1])
                    activate(p[:, P:3 * P], s[:, P:3 * P], ACT.Exp, bias=neg_max[:, h, 1:2],
                             accum_out=prob_sum[:, h, 1:2]).then_inc(exp_ready, 1)
                if h >= 1:
                    g = h - 1
                    act.wait_ge(pt_ps, g + 1)
                    if g >= 2:
                        act.wait_ge(o_ps, g - 1)
                    copy(probT[:, g % 2, :], bank[2 + g % 2][:, 0:3 * P]).then_inc(pt_ready, 1)
                    act.wait_ge(o_ps, g + 1)
                    copy(oT[:, g, :], bank[4 + g % 2][:, 0:T]).then_inc(o_ready, 1)
            rough_root(0)
            rough_root(1)
            for b in (4, 6):
                act.wait_ge(h1T_ps, b - 3)
                copy(h1T[:, 0:4, (b // 2 - 2) * P:(b // 2 - 1) * P],
                     bank[b][:, :].rearrange("p (c n) -> p c n", c=4)).then_inc(h1T_act, 1)
            act.wait_ge(top_ready, 1)
            for t in range(NT):
                last = activate(gate_e[:, t, :], top8[:, t, 0:TOPK], ACT.Exp, bias=gate_s[:, t:t + 1],
                                accum_out=gate_r[:, t:t + 1])
            last.then_inc(gexp_ready, 1)

            def take_tokens():
                copy(xeT.rearrange("p c n -> p (c n)"), bank[2][:, :]).then_inc(xe_ready, 1)

            act.sem_inc(y_ready, 1)
            act.sem_inc(selgT_ready, 1)
            act.wait_ge(gath_ps, 1)
            take_tokens()
            act.wait_ge(items_ready, 1)
            n_items = act.value_load(item_exp[0:1, ICOLS:ICOLS + 1], min_val=1, max_val=ITEMS)
            with act.Fori(0, ITEMS) as i:
                with act.If(i < n_items):
                    act.wait_ge(hg_ready, i + 1)
                    activate(sig, hg, ACT.Sigmoid, scale=SWI_ALPHA).then_inc(sig_ready, 1)
                    act.wait_ge(gath_ps, i + 2)
                    take_tokens()
                    act.wait_ge(actT_ps, i + 1)
                    copy(actT.rearrange("p c n -> p (c n)"), bank[3][:, :]).then_inc(actT_ready, 1)
                    act.wait_ge(selgT_ps, i + 1)
                    copy(selgT.rearrange("p c n -> p (c n)"), bank[2][:, 0:T]).then_inc(selgT_ready, 1)
                    act.wait_ge(w_used[5], i + 1)
                    copy(y_item, bank[1][:, :]).then_inc(y_ready, 1)

            def squares_at(start, size):
                return at(6160 + start, size)

            rough_root(2)
            rough_root(3)
            for t in range(NT):
                act.wait_ge(x2_ready, t + 1)
                activate(squares_at(t * D, D), x2[:, t, :], ACT.Square, accum_out=ss[:, t:t + 1]).then_inc(x_sq, 1)
            rough_root(4)
            rough_root(5)
            split_hi(IN2)
            evict_hi(0, 132)
            split_hi(IN2 + 1)
            for b in range(2):
                split_hi(IN2 + 2 + b)
                act.wait_ge(r2_ps, b + 1)
                z = zl[:, 2 * b:2 * b + 2, :].rearrange("p c n -> p (c n)")
                activate(z, bank[b][:, :], ACT.Abs).then_inc(f_abs, 1)
                act.wait_ge(f_abs, b + 1)
                link(activate(z, z, ACT.Exp, scale=-1.0))
                activate(z, z, ACT.Ln, bias=1.0).then_inc(f_log, 1)
            for b in range(2):
                act.wait_ge(lfm_ready, b + 1)
                z = k2[:, 2 * b:2 * b + 2, :]
                activate(z, z, ACT.Exp).then_inc(k_ready, 1)
            for b in range(2):
                split_hi(IN2 + 4 + b)
                act.wait_ge(r2_ps, 2 + b + 1)
                activate(kl[:, 2 * b:2 * b + 2, :].rearrange("p c n -> p (c n)"), bank[2 + b][:, :], ACT.Sigmoid
                         ).then_inc(q_sig, 1)

            def both_tiles(b):
                return bank[b][:, :].rearrange("p (t n) -> p t n", t=NT)

            for b in range(2):
                split_hi(IN2 + 6 + b)
                act.wait_ge(r2_ps, 4 + b + 1)
                copy(v2[:, :, b * 256:(b + 1) * 256], both_tiles(4 + b)).then_inc(v_ready, 1)
            for b in range(2):
                split_hi(IN2 + 8 + b)
                act.wait_ge(r2_ps, 6 + b + 1)
                activate(sg2[:, :, b * 256:(b + 1) * 256], both_tiles(6 + b), ACT.Sigmoid).then_inc(g_sig, 1)

            def decay(n):
                act.wait_ge(dec_ready, n + 1)
                activate(zl, zl, ACT.Exp).then_inc(z_ready, 1)

            def take(r, b, dst, done):
                act.wait_ge(r2_ps, r + 1)
                copy(dst[:, 2 * (b % 2):2 * (b % 2) + 2, :].rearrange("p c n -> p (c n)"), bank[b][:, :]
                     ).then_inc(done, 1)

            decay(0)
            for b in range(2):
                split_hi(IN2 + 10 + b)
                take(8 + b, b, gb, gb_ready)
            decay(1)
            split_hi(IN2 + 12)
            take(10, 2, gc, gc_ready)
            decay(2)
            decay(3)
            split_hi(IN2 + 13)
            take(11, 3, gc, gc_ready)
            for n in range(4, len(LEVELS) + 1):
                decay(n)
            act.wait_ge(o2_ps, 1)
            for t in range(NT):
                for h in range(HG):
                    last = activate(kl[:, h, t * P:(t + 1) * P], bank[t][:, h * P:(h + 1) * P], ACT.Square,
                                    accum_out=ss[:, 2 + t * HG + h:3 + t * HG + h])
            last.then_inc(o2_sq, 1)
            rough_root(6)
            for g in range(2):
                act.wait_ge(mT_ps, g + 1)
                for j in range(2):
                    h = 2 * g + j
                    activate(mixT[:, h, :], bank[6 + g][:, j * T:(j + 1) * T], ACT.Copy,
                             scale=vcol[:, 160 + h:161 + h]).then_inc(mT_ready, 1)

            def squares_of(ps, count, banks, done):
                for n, b in enumerate(banks):
                    if n % count == 0:
                        act.wait_ge(ps[0], ps[1](n))
                    last = activate(squares_at(n * 512, 512), bank[b][:, :], ACT.Square, accum_out=ss2[:, n:n + 1])
                    last.then_inc(done, 1)

            squares_of((mix_ps, lambda n: n + 2), 2, (2, 3, 4, 5), mix_sq)
            rough_root(7)
            rough_root(8)
            for t in range(NT):
                act.wait_ge(x3_ready, t + 1)
                activate(squares_at(t * D, D), x3[:, t, :], ACT.Square, accum_out=ss2[:, 4 + t:5 + t]).then_inc(x_sq, 1)
            rough_root(9)
            rough_root(10)
            split_hi(UP)
            evict_hi(4, 140)
            split_hi(UP + 1)

            def sigmoid_gate(f):
                act.wait_ge(cv_ready, f + 1)
                activate(sgt[:, f % 2, :], cv[:, f % 2, 0:T], ACT.Sigmoid).then_inc(up_sig, 1)

            def split_a_hi(p):
                act.wait_ge(a_ready, 2 * p + 2)
                if p == 0:
                    act.wait_ge(up_ps, FB)
                q = 2 * (p % 4)
                copy(x_hi[:, q:q + 2, :], aT[:, 2 * p:2 * p + 2, :]).then_inc(a_hi_ready, 1)

            for f in range(FB):
                act.wait_ge(up_ps, f + 1)
                if f == FB - 1:
                    split_a_hi(0)
                split_hi(UP + f + 2)
                if f >= 2:
                    act.wait_ge(a_ready, f - 1)
                u = up_sb[:, f % 2, :].rearrange("p (g n) -> p g n", g=2)
                for g in range(2):
                    col = 2 * 2 * FB + g * FB + f
                    last = activate(cv[:, f % 2, g * T:(g + 1) * T], bank[4 + f % 2][:, g * T:(g + 1) * T], ACT.Copy,
                                    scale=vcol[:, col:col + 1])
                last.then_inc(cv_tap, 1)
                copy(u[:, :, 2:T + 2], bank[4 + f % 2][:, :].rearrange("p (g n) -> p g n", g=2)
                     ).then_inc(up_ready, 1)
                if f >= 1:
                    sigmoid_gate(f - 1)
            split_a_hi(1)
            sigmoid_gate(FB - 1)
            for p in range(2, FB // 2):
                split_hi(DOWN + p)
                split_a_hi(p)
            act.wait_ge(down_ps, 1)
            squares_of((down_ps, lambda n: n // 2 + 1), 2, (0, 1, 2, 3), down_sq)
            rough_root(11)
            rough_root(12)

        @block.vector
        def _(dve):
            link = Link(dve, dve_step)
            tt, ts, stt = dve.tensor_tensor, dve.tensor_scalar, dve.scalar_tensor_tensor

            def split_lo(p):
                dve.wait_ge(hi_ready, p + 1)
                tt(like(w_lo, p), pieces[p][2], like(w_hi, p).bitcast(f32), ALU.subtract).then_inc(lo_ready, 1)

            def evict_lo(first, gain):
                for c in range(KC):
                    if c % 2 == 0:
                        dve.wait_ge(hT_hi, first + c + 2)
                    stt(x_lo[:, c, :], bank[c // 2][:, c % 2 * T:(c % 2 + 1) * T], vcol[:, gain + c:gain + c + 1],
                        x_hi[:, c, :].bitcast(f32), ALU.mult, ALU.subtract).then_inc(hT_lo, 1)

            for t in range(NT):
                for g in range(2):
                    b = 2 * t + g
                    dve.wait_ge(xT_hi, b + 1)
                    chunks, cols = slice(4 * g, 4 * g + 4), slice(t * P, (t + 1) * P)
                    tt(x_lo[:, chunks, cols], bank[b][:, :].rearrange("p (c n) -> p c n", c=4),
                       x_hi[:, chunks, cols].bitcast(f32), ALU.subtract).then_inc(xT_lo, 1)
            split_lo(IN1)
            split_lo(IN1 + 1)
            for r in range(12):
                if r % 2 == 0:
                    if r + 2 < 12:
                        split_lo(IN1 + r + 2)
                    continue
                if r == 9:
                    dve.wait_ge(rel_ps, 1)
                    tt(rel_tab, bank[0][0:H, :], behind_sb, ALU.add).then_inc(rel_ready, 1)
                    dve.wait_ge(vcol_ps, 1)
                    dve.tensor_copy(vcol[:, :], bank[1][:, 0:164]).then_inc(vcol_ready, 1)
                dve.wait_ge(proj_ps, r + 1)
                src = bank[(4 + r) % 8][:, :].rearrange("p (c n) -> p c n", c=2)
                if r < 8:
                    dst, h = (qT, r) if r < 4 else (kT, r - 4)
                    scale = float(P) ** -0.5 if r < 4 else 1.0
                    ts(dst[:, 2 * h:2 * h + 2, :], src, scale, None, ALU.mult).then_inc(proj_dve, 1)
                else:
                    dve.tensor_copy(v_tok[:, :, (r - 8) * 256:(r - 7) * 256], src).then_inc(proj_dve, 1)
                if r + 2 < 12:
                    split_lo(IN1 + r + 2)

            def row_max(h):
                dve.wait_ge(s_ps, h + 1)
                p = bank[h % 2]
                dve.tensor_reduce(neg_max[:, h, 0:1], p[:, 0:P], AX.X, ALU.max, negate=True)
                dve.tensor_reduce(neg_max[:, h, 1:2], p[:, P:3 * P], AX.X, ALU.max, negate=True
                                  ).then_inc(max_ready, 1)

            def normalise(h):
                dve.wait_ge(exp_ready, h + 1)
                p = prob[:, h % 2, :]
                link(dve.reciprocal(prob_inv[:, h, :], prob_sum[:, h, :]))
                ts(p[:, 0:P], p[:, 0:P], prob_inv[:, h, 0:1], None, ALU.mult)
                ts(p[:, P:3 * P], p[:, P:3 * P], prob_inv[:, h, 1:2], None, ALU.mult).then_inc(prob_ready, 1)

            row_max(0)
            for h in range(H):
                if h + 1 < H:
                    row_max(h + 1)
                normalise(h)

            def root_of(n, src, scale, eps):
                c, k = roots[n]
                ts(variance[:, c:c + k], src, scale, eps, ALU.mult, ALU.add).then_inc(var_ready, 1)

            def refine(n):
                c, k = roots[n]
                v, y, w = (a[:, c:c + k] for a in (variance, inv_root, newton))
                dve.wait_ge(rough_ready, n + 1)
                link(tt(w, y, y, ALU.mult))
                link(tt(w, w, v, ALU.mult))
                link(ts(w, w, -0.5, 1.5, ALU.mult, ALU.add))
                link(tt(y, y, w, ALU.mult))
                return y

            def root(n, src, scale, eps):
                root_of(n, src, scale, eps)
                return refine(n)

            def layer_norm(z, base, banks, n, done, ready):
                def moments_of(t):
                    dve.wait_ge(*done(t))
                    for g in range(2):
                        cols = slice(g * 512, (g + 1) * 512)
                        last = stt(z[:, t, cols], base[:, t, cols], ALPHA, banks[2 * g + t][:, :], ALU.mult, ALU.add)
                    link(last)
                    for g in range(2):
                        last = dve.bn_stats(stats[:, t, g, :], z[:, t, g * 512:(g + 1) * 512])
                    link(last)
                    link(dve.bn_aggr(moments[:, t, :], stats[:, t, :, :].rearrange("p a b -> p (a b)")))
                    root_of(n + t, moments[:, t, 1:2], 1.0, LN_EPS)

                def scale(t):
                    r = refine(n + t)
                    link(stt(z[:, t, :], z[:, t, :], moments[:, t, 0:1], row_g, ALU.subtract, ALU.mult))
                    stt(z[:, t, :], z[:, t, :], r, row_b, ALU.mult, ALU.add).then_inc(ready, 1)

                moments_of(0)
                moments_of(1)
                scale(0)
                scale(1)

            dve.wait_ge(ln0_in, 32)
            layer_norm(h1, x_tok, bank[0:4], 0, lambda t: (out_ps, 2 * t + 2), h1_ready)
            for b in (5, 7):
                dve.wait_ge(h1T_ps, b - 3)
                dve.tensor_copy(h1T[:, 4:8, (b // 2 - 2) * P:(b // 2 - 1) * P],
                                bank[b][:, :].rearrange("p (c n) -> p c n", c=4)).then_inc(h1T_dve, 1)

            dve.wait_ge(logit_ps, 1)
            for t in range(NT):
                last = tt(logit[:, t, :], bank[0][:, t * N_EXP:(t + 1) * N_EXP], br, ALU.add)
            link(last)
            for t in range(NT):
                last = dve.max(top8[:, t, :], logit[:, t, :])
            link(last)
            ts(gate_s, top8[:, :, 0], -1.0, None, ALU.mult).then_inc(top_ready, 1)
            for t in range(NT):
                last = dve.max_index(top_i[:, t, :], top8[:, t, :], logit[:, t, :])
            link(last)
            link(dve.tensor_copy(top_f, top_i))
            for t in range(NT):
                for k in range(TOPK):
                    last = ts(hit[:, t, k, :], const("expert"), top_f[:, t, k:k + 1], None, ALU.is_equal)
            link(last)
            link(dve.tensor_reduce(chosen, hit.rearrange("p t k e -> p t e k"), AX.X, ALU.add))
            dve.wait_ge(gexp_ready, 1)
            link(dve.reciprocal(gate_r, gate_r))
            for t in range(NT):
                last = ts(gate[:, t, :], gate_e[:, t, :], gate_r[:, t:t + 1], None, ALU.mult)
            link(last)
            for t in range(NT):
                last = ts(gates[:, t, :], hit[:, t, 0, :], gate[:, t, 0:1], None, ALU.mult)
            link(last)
            for k in range(1, TOPK):
                for t in range(NT):
                    last = stt(gates[:, t, :], hit[:, t, k, :], gate[:, t, k:k + 1], gates[:, t, :],
                               ALU.mult, ALU.add)
                if k < TOPK - 1:
                    link(last)
            last.then_inc(route_ready, 1)

            dve.wait_ge(pos_ps, 1)
            link(dve.tensor_copy(count, bank[2][0:N_EXP, 0:1]))
            link(ts(over, const("thresholds", N_EXP), count[:, 0:1], None, ALU.is_lt))
            link(dve.tensor_reduce(blocks, over, AX.X, ALU.add))
            link(stt(place.rearrange("p t e -> p (t e)"), bank[1][:, 0:2 * N_EXP], FAR,
                     chosen.rearrange("p t e -> p (t e)"), ALU.add, ALU.mult))
            link(ts(place, place, -FAR, None, ALU.add))
            link(dve.tensor_copy(gatesT, bank[3][0:N_EXP, 0:T]))
            tt(blocks, blocks, const("first", N_EXP), ALU.max).then_inc(blocks_ready, 1)
            dve.wait_ge(span_ps, 1)
            link(dve.tensor_copy(span, bank[0][:, 0:2]))
            link(ts(from_first, const("item"), span[:, 0:1], None, ALU.is_ge))
            link(ts(span64, span[0:N_EXP, 0:1], float(CAP), None, ALU.mult))
            link(ts(placeT, bank[1][0:N_EXP, 0:T], span64[:, 0:1], None, ALU.add))
            stt(owner, const("item"), span[:, 1:2], from_first, ALU.is_lt, ALU.mult).then_inc(owner_ready, 1)
            dve.wait_ge(items_ps, 1)
            for t in range(NT):
                tt(item_place[:, t, :], bank[2][:, t * ICOLS:(t + 1) * ICOLS], const("item64"), ALU.subtract)
            link(dve.tensor_copy(item_gate.rearrange("p t i -> p (t i)"), bank[3][:, 0:NT * ICOLS]))
            dve.tensor_copy(item_exp, bank[0][0:1, 0:ICOLS + 1]).then_inc(items_ready, 1)
            dve.wait_ge(items_ready, 1)

            places = const("slot")

            def select(i):
                for t in range(NT):
                    last = ts(sel[:, t, :], places[:, 0:CAP], item_place[:, t, bass.ds(i, 1)], None, ALU.is_equal)
                last.then_inc(sel_ready, 1)

            def select_bias(i):
                ts(bias_sel.rearrange("p q n -> p (q n)"), const("quarter"), owner[:, bass.ds(i, 1)], None,
                   ALU.mult).then_inc(bsel_ready, 1)

            select(0)
            select_bias(0)
            dve.sem_inc(gu_read, 1)
            n_items = dve.value_load(item_exp[0:1, ICOLS:ICOLS + 1], min_val=1, max_val=ITEMS)
            with dve.Fori(0, ITEMS) as i:
                with dve.If(i < n_items):
                    dve.wait_ge(gath_ps, i + 1)
                    select(i + 1)
                    dve.wait_ge(selgT_ready, i + 1)
                    for t in range(NT):
                        last = ts(selg[:, t, :], places, item_place[:, t, bass.ds(i, 1)],
                                  item_gate[:, t, bass.ds(i, 1)], ALU.is_equal, ALU.mult)
                    last.then_inc(selg_ready, 1)
                    dve.wait_ge(w_used[3], i + 1)
                    ts(hg, bank[0][:, :], SWI_LIMIT, None, ALU.min).then_inc(hg_ready, 1)
                    ts(hu, bank[1][:, :], SWI_LIMIT, -SWI_LIMIT, ALU.min, ALU.max).then_inc(gu_read, 1)
                    select_bias(i + 1)
                    dve.wait_ge(gu_read, i + 2)
                    stt(hu, hu, 1.0, hg, ALU.add, ALU.mult).then_inc(prod_ready, 1)
                    dve.wait_ge(prod_ready, i + 1)
                    dve.wait_ge(sig_ready, i + 1)
                    tt(act_e.rearrange("p c n -> p (c n)"), hu, sig, ALU.mult).then_inc(act_ready, 1)

            dve.wait_ge(moe_done, 1)
            dve.wait_ge(ln1_in, 32)
            layer_norm(x2, h1, bank[4:8], 2, lambda t: (moe_done, 1), x2_ready)

            for t in range(NT):
                dve.wait_ge(x_sq, t + 1)
                r = root(4 + t, ss[:, t:t + 1], 1.0 / D, RMS_EPS)
                ts(xn[:, t, :], x2[:, t, :], r, None, ALU.mult).then_inc(xn_ready, 1)
            split_lo(IN2)
            evict_lo(0, 132)
            split_lo(IN2 + 1)
            marks = ql.rearrange("p h t -> p (h t)")
            link(dve.memset(marks, 1.0))
            link(dve.memset(marks[:, 0:HG * T:64], 0.0))
            link(dve.memset(att, 0.0))
            split_lo(IN2 + 2)
            for b in range(2):
                dve.wait_ge(f_log, b + 1)
                cols = slice(2 * b, 2 * b + 2)
                dst = lf[:, cols, :].rearrange("p c n -> p (c n)")
                link(stt(dst, bank[b][:, :], 0.0, zl[:, cols, :].rearrange("p c n -> p (c n)"),
                         ALU.min, ALU.subtract))
                tt(k2[:, cols, :].rearrange("p c n -> p (c n)"), dst, bank[b][:, :], ALU.subtract
                   ).then_inc(lfm_ready, 1)
                if b == 0:
                    split_lo(IN2 + 3)
            flat = lf.rearrange("p h t -> p (h t)")
            link(dve.tensor_tensor_scan(cum.rearrange("p h t -> p (h t)"), marks, flat, 0.0, ALU.mult, ALU.add))
            link(dve.memset(marks[:, 64:HG * T:128], 1.0))
            link(dve.tensor_tensor_scan(cum2.rearrange("p h t -> p (h t)"), marks, flat, 0.0, ALU.mult, ALU.add))

            def squares(buffer, n):
                return buffer.rearrange("p h t -> p (h t)").rearrange("p (a b) -> p a b", b=2 * LEVELS[n])

            def decays(n):
                src, dst = squares(cum if LEVELS[n] < 64 else cum2, n), squares(zl, n)
                m = LEVELS[n]
                mid = src[:, :, m - 1:m].to_broadcast([P, HG * T // (2 * m), m])
                tt(dst[:, :, 0:m], mid, src[:, :, 0:m], ALU.subtract)
                tt(dst[:, :, m:2 * m], src[:, :, m:2 * m], mid, ALU.subtract).then_inc(dec_ready, 1)

            decays(0)
            split_lo(IN2 + 4)
            for b in range(2):
                dve.wait_ge(q_sig, b + 1)
                cols = slice(2 * b, 2 * b + 2)
                stt(q2[:, cols, :].rearrange("p c n -> p (c n)"), bank[2 + b][:, :], float(P) ** -0.5,
                    kl[:, cols, :].rearrange("p c n -> p (c n)"), ALU.mult, ALU.mult).then_inc(q_ready, 1)
                split_lo(IN2 + 6 + b - 1)
            split_lo(IN2 + 7)
            split_lo(IN2 + 8)
            for b in range(2):
                dve.wait_ge(g_sig, b + 1)
                half = sg2[:, :, b * 256:(b + 1) * 256]
                tt(half, half, bank[6 + b][:, :].rearrange("p (t n) -> p t n", t=NT), ALU.mult).then_inc(g_ready, 1)
                split_lo(IN2 + 9 + b)
            split_lo(IN2 + 11)
            dve.wait_ge(q_ready, 2)
            dve.wait_ge(lev_in, 16)

            def keep(n):
                for b in range(2):
                    dve.wait_ge(lv_ps, 2 * n + b + 1)
                    mask = lev[:, n:n + 1, :].to_broadcast([P, 4, P]).bitcast(u32)
                    last = dve.copy_predicated(att[:, 4 * b:4 * b + 4, :], mask,
                                               bank[6 + b][:, :].rearrange("p (a n) -> p a n", a=4))
                last.then_inc(lv_ready, 1)

            def decayed(n):
                m = LEVELS[n]
                dve.wait_ge(z_ready, n + 1)
                tt(squares(kl, n)[:, :, 0:m], squares(k2, n)[:, :, 0:m], squares(zl, n)[:, :, 0:m], ALU.mult)
                tt(squares(ql, n)[:, :, m:2 * m], squares(q2, n)[:, :, m:2 * m], squares(zl, n)[:, :, m:2 * m],
                   ALU.mult).then_inc(ql_ready, 1)
                dve.wait_ge(ql_ready, n + 1)

            for n in range(len(LEVELS)):
                if n:
                    dve.wait_ge(lv_ps, 2 * n + 2)
                decayed(n)
                if n + 1 < len(LEVELS):
                    decays(n + 1)
                else:
                    link(tt(zl[:, :, 0:P], cum2[:, :, P - 1:P].to_broadcast([P, HG, P]), cum2[:, :, 0:P],
                            ALU.subtract))
                    dve.tensor_copy(zl[:, :, P:T], cum2[:, :, P:T]).then_inc(dec_ready, 1)
                keep(n)
                if n in (1, 3):
                    split_lo(IN2 + 12 + n // 2)
            n = len(LEVELS)
            dve.wait_ge(lv_ps, 2 * n + 2)
            dve.wait_ge(z_ready, n + 1)
            tt(kl[:, :, 0:P], k2[:, :, 0:P], zl[:, :, 0:P], ALU.mult)
            tt(ql[:, :, P:T], q2[:, :, P:T], zl[:, :, P:T], ALU.mult).then_inc(ql_ready, 1)
            keep(n)
            link(dve.memset(cm[:, :, 0:2], 0.0))
            dve.wait_ge(gc_ready, 2)
            for b in range(2):
                dve.wait_ge(r2_ps, 12 + b + 1)
                cols = slice(2 * b, 2 * b + 2)
                link(tt(cm[:, cols, 2:T + 2], gc[:, cols, :], bank[4 + b][:, :].rearrange("p (c n) -> p c n", c=2),
                        ALU.mult))
            dve.wait_ge(lv_ps, 2 * n + 3)
            dve.tensor_copy(att2.rearrange("p h n -> p (h n)"), bank[2][:, :]).then_inc(lv_ready, 1)
            dve.wait_ge(gb_ready, 2)
            for j in range(3):
                for c in range(CB):
                    w = vcol[:, 148 + j * CB + c:149 + j * CB + c]
                    if j == 0:
                        last = ts(gc[:, c, :], cm[:, c, 0:T], w, None, ALU.mult)
                    else:
                        last = stt(gc[:, c, :], cm[:, c, j:j + T], w, gc[:, c, :], ALU.mult, ALU.add)
                link(last)
            for c in range(CB):
                tt(gb[:, c, :], gb[:, c, :], gc[:, c, :], ALU.mult).then_inc(conv_ready, 1)
            dve.wait_ge(o2_sq, 1)
            dve.wait_ge(g_ready, 2)
            r = root(6, ss[:, 2:10], 1.0 / P, RMS_EPS)
            for t in range(NT):
                for h in range(HG):
                    cols = slice(h * P, (h + 1) * P)
                    last = stt(o_tok[:, t, cols], bank[t][:, cols], r[:, t * HG + h:t * HG + h + 1],
                               sg2[:, t, cols], ALU.mult, ALU.mult)
            last.then_inc(o2_ready, 1)

            def rms_residual(n, t, sums, banks, gain, base, dst, ready):
                link(tt(sq_sum[:, t:t + 1], sums[0], sums[1], ALU.add))
                r = root(n, sq_sum[:, t:t + 1], 1.0 / D, RMS_EPS)
                for g in range(2):
                    cols = slice(g * 512, (g + 1) * 512)
                    last = stt(dst[:, t, cols], bank[banks[g]][:, :], r, gain[:, cols],
                               ALU.mult, ALU.mult)
                link(last)
                tt(dst[:, t, :], dst[:, t, :], base[:, t, :], ALU.add).then_inc(ready, 1)

            dve.wait_ge(post_in, 32)
            for t in range(NT):
                dve.wait_ge(mix_sq, 2 * t + 2)
                rms_residual(7 + t, t, (ss2[:, 2 * t:2 * t + 1], ss2[:, 2 * t + 1:2 * t + 2]), (2 + 2 * t, 3 + 2 * t), post_g, x2, x3,
                             x3_ready)
            for t in range(NT):
                dve.wait_ge(x_sq, NT + t + 1)
                r = root(9 + t, ss2[:, 4 + t:5 + t], 1.0 / D, RMS_EPS)
                ts(xn[:, t, :], x3[:, t, :], r, None, ALU.mult).then_inc(xn_ready, 1)
            split_lo(UP)
            evict_lo(KC, 140)
            split_lo(UP + 1)
            for b in range(2):
                u = up_sb[:, b, :].rearrange("p (g n) -> p g n", g=2)
                link(dve.memset(u[:, :, 0:2], 0.0))

            def split_a_lo(p):
                dve.wait_ge(a_hi_ready, p + 1)
                q = 2 * (p % 4)
                tt(x_lo[:, q:q + 2, :], aT[:, 2 * p:2 * p + 2, :], x_hi[:, q:q + 2, :].bitcast(f32), ALU.subtract
                   ).then_inc(a_lo_ready, 1)

            for f in range(FB):
                if f == FB - 1:
                    split_a_lo(0)
                split_lo(UP + f + 2)
                dve.wait_ge(cv_tap, f + 1)
                dve.wait_ge(up_ready, f + 1)
                u = up_sb[:, f % 2, :].rearrange("p (g n) -> p g n", g=2)
                y = cv[:, f % 2, :].rearrange("p (g n) -> p g n", g=2)
                for j in range(2):
                    for g in range(2):
                        col = j * 2 * FB + g * FB + f
                        last = stt(y[:, g, :], u[:, g, j:j + T], vcol[:, col:col + 1], y[:, g, :], ALU.mult, ALU.add)
                    if j == 0:
                        link(last)
                last.then_inc(cv_ready, 1)
            split_a_lo(1)
            for p in range(2, FB // 2):
                split_lo(DOWN + p)
                split_a_lo(p)
            for t in range(NT):
                dve.wait_ge(down_sq, 2 * t + 2)
                rms_residual(11 + t, t, (ss2[:, 2 * t:2 * t + 1], ss2[:, 2 * t + 1:2 * t + 2]), (2 * t, 2 * t + 1), post_b, x3,
                             y_out, y_done)


_USED = ("x", "rel_bias", "a_w_in", "a_w_out", "ln_g", "ln_b", "moe_w_router", "moe_b_router", "moe_w_gate_up",
         "moe_b_gate_up", "moe_w_down", "moe_b_down", "w_in_2", "w_out_2", "conv_w_2", "ffn_w_up_2",
         "ffn_conv_w_2", "ffn_w_down_2", "hgrn_norm_g_2", "pre_mix_g_2", "post_mix_g_2", "pre_ffn_g_2",
         "post_ffn_g_2")
_WHOLE = ("rel_bias",)


def kernel(**inputs):
    import concourse.bacc as bacc
    from concourse.bass_utils import run_bass_kernel_spmd

    nc = bacc.Bacc("TRN2", target_bir_lowering=False, num_devices=1)
    arrays, args = {}, []
    for name in _USED:
        a = np.ascontiguousarray(inputs[name])
        arrays[f"in_{name}"] = a
        ap = nc.dram_tensor(f"in_{name}", a.shape, mybir.dt.from_np(a.dtype), kind="ExternalInput").ap()
        args.append(ap if name in _WHOLE else ap[0])
    for name, a in zip(("consts", "levels", "buckets", "behind"), shape_constants()):
        arrays[f"in_{name}"] = a
        args.append(nc.dram_tensor(f"in_{name}", a.shape, mybir.dt.float32, kind="ExternalInput").ap())
    args.append(nc.dram_tensor("rel_rows", (H, 2 * T), mybir.dt.float32, kind="Internal").ap())
    args.append(nc.dram_tensor("out", (1, T, D), mybir.dt.float32, kind="ExternalOutput").ap()[0])
    build(nc, *args)
    r = run_bass_kernel_spmd(nc, [arrays], core_ids=[0])
    return r.results[0]["out"]
```
